# Optimizing a Trainium2 kernel written in Bass

```python
import math
import jax
import jax.numpy as jnp
from jax import lax
import numpy as np

D_MODEL = 2048
BATCH = 1
SEQ = 256
DEPTH = 2

HEAD_DIM = 128
DN_HEADS = 6
DN_CONV = 4
DN_CHUNK = 64
POOL_WINDOWS = (2, 4, 8, 16)
POOL_GROUPS = 4
POOL_GROUP_DIM = 128
SWA_HEADS = 6
SWA_KV_HEADS = 2
SWA_WINDOW = 128
SWA_BLOCK = 128
ROPE_THETA = 10000.0
D_FF = 5632
FFN_CONV = 3
NORM_EPS = 1e-6

DN_W = DN_HEADS * HEAD_DIM
POOL_W = POOL_GROUPS * POOL_GROUP_DIM
SWA_W = SWA_HEADS * HEAD_DIM
SWA_KV_W = SWA_KV_HEADS * HEAD_DIM
MIX_W = DN_W + POOL_W + SWA_W
IN_SIZES = (3 * DN_W, DN_W, DN_HEADS, DN_HEADS, POOL_W, SWA_W, SWA_KV_W, SWA_KV_W)
IN_W = int(sum(IN_SIZES))
IN_OFFSETS = tuple(int(v) for v in np.cumsum(IN_SIZES)[:-1])

kernel_name = "hybrid_parallel_heads_deltanet_pool_swa"

def rms_norm(x, w):
    xf = x.astype(jnp.float32)
    y = xf * lax.rsqrt(jnp.mean(xf * xf, axis=-1, keepdims=True) + NORM_EPS)
    return (y * w.astype(jnp.float32)).astype(x.dtype)

def l2_norm(x):
    return x * lax.rsqrt(jnp.sum(x * x, axis=-1, keepdims=True) + NORM_EPS)

def causal_dwconv(x, w):
    K = w.shape[0]
    T = x.shape[1]
    xp = jnp.pad(x, ((0, 0), (K - 1, 0), (0, 0)))
    return sum(xp[:, k:k + T] * w[k] for k in range(K))

def rope(x, cos, sin):
    xf = x.astype(jnp.float32)
    x1, x2 = jnp.split(xf, 2, axis=-1)
    return jnp.concatenate([x1 * cos - x2 * sin, x2 * cos + x1 * sin], axis=-1).astype(x.dtype)

def unit_lower_inverse(lmat):
    C = lmat.shape[-1]
    eye = jnp.eye(C, dtype=jnp.float32)
    nil = -lmat
    inv = eye + nil
    powk = nil
    for _ in range(int(math.log2(C)) - 1):
        powk = jnp.matmul(powk, powk)
        inv = jnp.matmul(inv, eye + powk)
    return inv

def chunk_gated_delta_rule(q, k, v, g, beta):
    B, T, H, D = q.shape
    C = DN_CHUNK
    N = T // C
    q, k, v = (t.reshape(B, N, C, H, D) for t in (q, k, v))
    g = g.reshape(B, N, C, H)
    beta = beta.reshape(B, N, C, H)
    gc = jnp.cumsum(g, axis=2)
    gct = jnp.moveaxis(gc, 2, 3)
    idx = jnp.arange(C)
    causal = idx[:, None] >= idx[None, :]
    strict = idx[:, None] > idx[None, :]
    decay = jnp.exp(jnp.where(causal, gct[..., :, None] - gct[..., None, :], -jnp.inf))
    kb = k * beta[..., None]
    vb = v * beta[..., None]
    lmat = jnp.where(strict, jnp.einsum('bnihd,bnjhd->bnhij', kb, k) * decay, 0.0)
    tinv = unit_lower_inverse(lmat)
    eg = jnp.exp(gc)[..., None]
    u = jnp.einsum('bnhij,bnjhd->bnihd', tinv, vb)
    w = jnp.einsum('bnhij,bnjhd->bnihd', tinv, kb * eg)
    a_intra = jnp.einsum('bnihd,bnjhd->bnhij', q, k) * decay
    g_last = gc[:, :, -1:, :]
    q_dec = q * eg
    k_dec = k * jnp.exp(g_last - gc)[..., None]
    cdec = jnp.exp(g_last[:, :, 0, :])

    def step(S, xs):
        u_n, w_n, q_n, k_n, a_n, c_n = xs
        v_new = u_n - jnp.einsum('bchk,bhkv->bchv', w_n, S)
        o_n = jnp.einsum('bchk,bhkv->bchv', q_n, S) + jnp.einsum('bhij,bjhv->bihv', a_n, v_new)
        S = S * c_n[:, :, None, None] + jnp.einsum('bchk,bchv->bhkv', k_n, v_new)
        return S, o_n

    xs = tuple(jnp.moveaxis(t, 1, 0) for t in (u, w, q_dec, k_dec, a_intra, cdec))
    S0 = jnp.zeros((B, H, D, D), jnp.float32)
    _, o = lax.scan(step, S0, xs)
    return jnp.moveaxis(o, 0, 1).reshape(B, T, H, D)

def gated_deltanet(p_qkv, p_z, p_b, p_a, conv_w, a_log, dt_bias, norm_w):
    B, T, _ = p_qkv.shape
    f32 = jnp.float32
    qkv = jax.nn.silu(causal_dwconv(p_qkv, conv_w)).astype(f32)
    q, k, v = jnp.split(qkv, 3, axis=-1)
    shp = (B, T, DN_HEADS, HEAD_DIM)
    q = l2_norm(q.reshape(shp)) * (HEAD_DIM ** -0.5)
    k = l2_norm(k.reshape(shp))
    v = v.reshape(shp)
    beta = jax.nn.sigmoid(p_b.astype(f32))
    g = -jnp.exp(a_log.astype(f32)) * jax.nn.softplus(p_a.astype(f32) + dt_bias.astype(f32))
    o = chunk_gated_delta_rule(q, k, v, g, beta)
    o = rms_norm(o, norm_w) * jax.nn.silu(p_z.astype(f32).reshape(shp))
    return o.reshape(B, T, DN_W).astype(p_qkv.dtype)

def multiscale_pool(p_pool, pool_w, pool_scale):
    B, T, _ = p_pool.shape
    xg = p_pool.astype(jnp.float32).reshape(B, T, POOL_GROUPS, POOL_GROUP_DIM)
    cs = jnp.cumsum(xg, axis=1)
    t = jnp.arange(T)
    outs = []
    for gi, win in enumerate(POOL_WINDOWS):
        c = cs[:, :, gi]
        prev = jnp.pad(c, ((0, 0), (win, 0), (0, 0)))[:, :T]
        cnt = jnp.minimum(t + 1, win).astype(jnp.float32)
        outs.append((c - prev) / cnt[None, :, None] - xg[:, :, gi])
    y = jnp.stack(outs, axis=2)
    y = jnp.einsum('btgc,gcd->btgd', y, pool_w.astype(jnp.float32))
    return (y.reshape(B, T, POOL_W) * pool_scale.astype(jnp.float32)).astype(p_pool.dtype)

def band_blocks(t, blk):
    B, T = t.shape[:2]
    nb = T // blk
    tp = jnp.pad(t, ((0, 0), (blk, 0), (0, 0), (0, 0))).reshape(B, nb + 1, blk, *t.shape[2:])
    return jnp.concatenate([tp[:, :-1], tp[:, 1:]], axis=2)

def band_mask(nb, blk):
    ii = jnp.arange(blk)[:, None]
    jj = jnp.arange(2 * blk)[None, :]
    diff = blk + ii - jj
    in_win = (diff >= 0) & (diff < SWA_WINDOW)
    blk_idx = jnp.arange(nb)[:, None, None]
    return in_win[None] & ((blk_idx > 0) | (jj >= blk)[None])

def swa_sink_attention(p_q, p_k, p_v, sinks, cos, sin):
    B, T, _ = p_q.shape
    G = SWA_HEADS // SWA_KV_HEADS
    bq = SWA_BLOCK
    nb = T // bq
    q = rope(p_q.reshape(B, T, SWA_HEADS, HEAD_DIM), cos, sin)
    k = rope(p_k.reshape(B, T, SWA_KV_HEADS, HEAD_DIM), cos, sin)
    v = p_v.reshape(B, T, SWA_KV_HEADS, HEAD_DIM)
    qb = q.reshape(B, nb, bq, SWA_KV_HEADS, G, HEAD_DIM)
    kb = band_blocks(k, bq)
    vb = band_blocks(v, bq)
    s = jnp.einsum('bnihgd,bnjhd->bnhgij', qb, kb, preferred_element_type=jnp.float32) * (HEAD_DIM ** -0.5)
    s = jnp.where(band_mask(nb, bq)[None, :, None, None], s, -jnp.inf)
    sink = jnp.broadcast_to(
        sinks.astype(jnp.float32).reshape(SWA_KV_HEADS, G)[None, None, :, :, None, None],
        s.shape[:-1] + (1,))
    p = jax.nn.softmax(jnp.concatenate([s, sink], axis=-1), axis=-1)[..., :-1]
    o = jnp.einsum('bnhgij,bnjhd->bnihgd', p.astype(v.dtype), vb)
    return o.reshape(B, T, SWA_W)

def conv_glu_ffn(h, w_up, conv_w, conv_b, w_down):
    u = causal_dwconv(h @ w_up, conv_w) + conv_b
    a, b = jnp.split(u, 2, axis=-1)
    return (jax.nn.silu(a) * b) @ w_down

def setup_inputs(seed: int = 0) -> dict:
    key = jax.random.key(seed)
    ks = jax.random.split(key, 24)
    f32 = jnp.float32

    def nrm(k, shape, scale):
        return jax.random.normal(k, shape, f32) * scale

    def gain(k, shape):
        return 1.0 + 0.02 * jax.random.normal(k, shape, f32)

    x = jax.random.normal(ks[0], (BATCH, SEQ, D_MODEL), f32)
    offs = jax.random.randint(ks[1], (BATCH, 1), 0, 1024)
    positions = (offs + jnp.arange(SEQ)[None, :]).astype(jnp.int32)
    dt = jnp.exp(jax.random.uniform(ks[2], (DEPTH, DN_HEADS), f32, math.log(1e-3), math.log(1e-1)))
    return {
        "x": x,
        "positions": positions,
        "norm_mix_pre": gain(ks[3], (DEPTH, D_MODEL)),
        "w_in": nrm(ks[4], (DEPTH, D_MODEL, IN_W), D_MODEL ** -0.5),
        "dn_conv_w": nrm(ks[5], (DEPTH, DN_CONV, 3 * DN_W), DN_CONV ** -0.5),
        "dn_a_log": jnp.log(jax.random.uniform(ks[6], (DEPTH, DN_HEADS), f32, 1.0, 16.0)),
        "dn_dt_bias": dt + jnp.log(-jnp.expm1(-dt)),
        "dn_norm_w": gain(ks[7], (DEPTH, HEAD_DIM)),
        "pool_w": nrm(ks[8], (DEPTH, POOL_GROUPS, POOL_GROUP_DIM, POOL_GROUP_DIM), POOL_GROUP_DIM ** -0.5),
        "pool_scale": gain(ks[9], (DEPTH, POOL_W)),
        "swa_sinks": nrm(ks[10], (DEPTH, SWA_HEADS), 1.0),
        "w_out": nrm(ks[11], (DEPTH, MIX_W, D_MODEL), MIX_W ** -0.5),
        "norm_mix_post": gain(ks[12], (DEPTH, D_MODEL)),
        "norm_ffn_pre": gain(ks[13], (DEPTH, D_MODEL)),
        "ffn_w_up": nrm(ks[14], (DEPTH, D_MODEL, 2 * D_FF), D_MODEL ** -0.5),
        "ffn_conv_w": nrm(ks[15], (DEPTH, FFN_CONV, 2 * D_FF), FFN_CONV ** -0.5),
        "ffn_conv_b": nrm(ks[16], (DEPTH, 2 * D_FF), 0.01),
        "ffn_w_down": nrm(ks[17], (DEPTH, D_FF, D_MODEL), D_FF ** -0.5),
        "norm_ffn_post": gain(ks[18], (DEPTH, D_MODEL)),
    }

def reference(x, positions, norm_mix_pre, w_in, dn_conv_w, dn_a_log, dn_dt_bias, dn_norm_w,
              pool_w, pool_scale, swa_sinks, w_out, norm_mix_post, norm_ffn_pre,
              ffn_w_up, ffn_conv_w, ffn_conv_b, ffn_w_down, norm_ffn_post):
    inv_freq = 1.0 / (ROPE_THETA ** (jnp.arange(0, HEAD_DIM, 2, dtype=jnp.float32) / HEAD_DIM))
    ang = positions.astype(jnp.float32)[..., None] * inv_freq
    cos = jnp.cos(ang)[:, :, None, :]
    sin = jnp.sin(ang)[:, :, None, :]
    for l in range(DEPTH):
        h = rms_norm(x, norm_mix_pre[l])
        p = h @ w_in[l]
        dn_qkv, dn_z, dn_b, dn_a, p_pool, sq, sk, sv = jnp.split(p, IN_OFFSETS, axis=-1)
        y_dn = gated_deltanet(dn_qkv, dn_z, dn_b, dn_a, dn_conv_w[l], dn_a_log[l], dn_dt_bias[l], dn_norm_w[l])
        y_pool = multiscale_pool(p_pool, pool_w[l], pool_scale[l])
        y_swa = swa_sink_attention(sq, sk, sv, swa_sinks[l], cos, sin)
        mix = jnp.concatenate([y_dn, y_pool, y_swa], axis=-1) @ w_out[l]
        x = x + rms_norm(mix, norm_mix_post[l])
        h = rms_norm(x, norm_ffn_pre[l])
        f = conv_glu_ffn(h, ffn_w_up[l], ffn_conv_w[l], ffn_conv_b[l], ffn_w_down[l])
        x = x + rms_norm(f, norm_ffn_post[l])
    return x


_drawn_inputs = setup_inputs


def setup_inputs(seed=0):
    import zlib

    import numpy as np

    out = dict(_drawn_inputs(seed))
    spreads = {}
    factors = {'dn_norm_w': 3.948, 'pool_scale': 3.342, 'ffn_conv_b': 4.825, 'norm_ffn_post': 3.385}
    for name, (base, spread) in spreads.items():
        noise = np.random.default_rng([zlib.crc32(name.encode()), seed]).standard_normal(out[name].shape)
        drawn = base * np.exp(spread * noise) if base else spread * noise
        out[name] = jnp.asarray(drawn.astype(out[name].dtype))
    for name, factor in factors.items():
        out[name] = (out[name] * factor).astype(out[name].dtype)
    return out
```

```python
from contextlib import ExitStack

import concourse.bass as bass
import numpy as np
from concourse import mybir

F32 = mybir.dt.float32
F32R = mybir.dt.float32r
I32 = mybir.dt.int32
ALU = mybir.AluOpType
ACT = mybir.ActivationFunctionType
AX = mybir.AxisListType

P = 128
D = 2048
T = 256
TT = T // P
KT = D // P
DEPTH = 2
HD = 128
DN_H = 6
DN_TILES = 3 * DN_H
DN_TAPS = 4
CH = 64
NG = 3
WINDOWS = (2, 4, 8, 16)
NPOOL = 4
SWA_H, SWA_KV = 6, 2
REP = SWA_H // SWA_KV
FF = 5632
FT = FF // P
FFN_TAPS = 3
EPS = 1e-6
QSCALE = HD ** -0.5
MAGIC = 12582912.0

COL_Z = 3 * DN_H * HD
COL_BA = COL_Z + DN_H * HD
COL_POOL = COL_BA + 2 * DN_H
COL_SQ = COL_POOL + NPOOL * P
COL_SK = COL_SQ + SWA_H * HD
COL_SV = COL_SK + SWA_KV * HD
NBA = 2 * DN_H

GATE_PAIR = 9
N_IN, N_OUT, N_UP, N_DOWN = 20, KT // 2, 2 * FT // 2, FT // 2
P_IN, P_OUT, P_UP, P_DOWN = 0, N_IN, N_IN + N_OUT, N_IN + N_OUT + N_UP
PAIRS = P_DOWN + N_DOWN
SUBS = 4 * PAIRS
TAIL = ([(COL_Z + 256 * i, 34 + 2 * i) for i in range(3)] + [(COL_SK, 40), (COL_SV, 42)]
        + [(COL_POOL + 256 * i, 6 + 2 * i) for i in range(2)]
        + [(COL_SQ + 256 * i, 10 + 2 * i) for i in range(3)])
T_POOL, T_SQ, T_QKV, T_Z, T_SK, T_SV = 6, 10, 16, 34, 40, 42

R_PRE, R_FFN, R_DNC, R_PS = 0, KT, 2 * KT, 2 * KT + DN_TAPS * DN_TILES
R_DNW = R_PS + NPOOL
R_ONE = R_DNW + 1
R_FC = R_ONE
R_FB = R_FC + FFN_TAPS * 2 * FT
R_ALL = R_FB + 2 * FT
FROWS = R_ALL - R_ONE

C_ID, C_U, C_LS, C_BD = 0, P, 2 * P, 3 * P
C_SWA = 4 * P
C_COR = C_SWA + 3 * P
C_INVF = C_COR + NPOOL * 16
C_SGN = C_INVF + 1
C_ALL = C_SGN + 1


def constants():
    c = np.zeros((P, C_ALL), np.float32)
    i, j = np.arange(P)[:, None], np.arange(P)[None, :]
    same = (i // CH) == (j // CH)
    c[:, C_ID:C_ID + P] = i == j
    c[:, C_U:C_U + P] = same & (i <= j)
    c[:, C_LS:C_LS + P] = same & (i > j)
    c[:, C_BD:C_BD + P] = same
    far = np.float32(-1e30)
    c[:, C_SWA:C_SWA + P] = np.where(j <= i, 0, far)
    c[:, C_SWA + P:C_SWA + 2 * P] = np.where(j > i, 0, far)
    c[:, C_SWA + 2 * P:C_SWA + 3 * P] = np.where(j <= i, 0, far)
    for g, w in enumerate(WINDOWS):
        c[:, C_COR + 16 * g:C_COR + 16 * (g + 1)] = w / np.minimum(np.arange(16) + 1, w)
    freq = (1.0 / np.float32(10000.0) ** (np.arange(0, HD, 2, dtype=np.float32) / np.float32(HD))).astype(np.float32)
    c[:, C_INVF] = np.concatenate([freq, freq])
    c[:, C_SGN] = np.where(np.arange(P) < HD // 2, 1, -1)
    return c


def trunk(nc, a, out):
    with ExitStack() as ctx:
        def sb(name, shape, dt=F32):
            return ctx.enter_context(nc.sbuf_tensor(name, shape, dt))

        used = {}

        def sem(name):
            if name not in used:
                used[name] = ctx.enter_context(nc.semaphore(name))
            return used[name]

        x = sb("x", [P, TT, D])
        h_hi = sb("h_hi", [P, KT, T], F32R)
        h_lo = sb("h_lo", [P, KT, T], F32R)
        raw = sb("raw", [P, 2, 4096])
        w_hi = sb("w_hi", [P, 4, 1024], F32R)
        w_lo = sb("w_lo", [P, 4, 1024], F32R)
        act_t = sb("act_t", [P, FT, T])
        scr = sb("scratch", [P, 18, 512])
        const = sb("const", [P, C_ALL])
        cos_t = sb("cos_t", [P, T])
        sin_t = sb("sin_t", [P, T])
        rows1 = sb("rows1", [P, P])
        rows2 = sb("rows2", [P, 3, P])
        par = sb("par", [P, R_ALL])
        pool_w = sb("pool_w", [P, NPOOL, P])
        heads = sb("heads", [P, 3, DN_H])
        small = sb("small", [P, 64])
        gate = sb("gate", [P, 7, DN_H, TT])
        gate_g = sb("gate_g", [P, 7, 4])
        gtmp = sb("gtmp", [P, 4, DN_H, TT])
        ba = sb("ba", [P, TT, NBA])
        vec = sb("vec", [P, 11, 4])
        soft = sb("soft", [P, 4, REP, 2])
        mhalf = sb("mhalf", [P, 16])
        ps = ctx.enter_context(nc.psum_tensor("ps", [P, 8, 512], F32))

        ident = const[:, C_ID:C_ID + P]
        upper = const[:, C_U:C_U + P]
        lower = const[:, C_LS:C_LS + P]
        block = const[:, C_BD:C_BD + P]

        h_tok = scr[:, 0:8, :].rearrange("p a (b n) -> p (a b n)", b=1).rearrange("p (t d) -> p t d", t=TT)
        w_post = scr[:, 8:12, :]
        y_ab = scr[:, 16:18, :].rearrange("p a (b n) -> p a b n", b=2)
        (q_s, k_s, v_s, z_s, qn, qd, kn, kbeg, kdec, vb, kn_t, qn_t, qd_t, e1, e2, vs, gb) = (
            scr[:, i, :] for i in range(17))
        pw, pw_t, inv, attn, u_m, w_t, o_m = q_s, k_s, v_s, qn, qd, kn, e1
        v_new, state = vs[:, 0:256], vs[:, 256:512]
        rope_x, roped = scr[:, 0:2, :].rearrange("p a (b n) -> p (a b) n", n=T), scr[:, 2:4, :].rearrange("p a (b n) -> p (a b) n", n=T)
        v_st, v_tok = scr[:, 4, 0:T], scr[:, 5, 0:T]
        prob, prob_t = scr[:, 6:9, 0:3 * P], scr[:, 9:12, 0:3 * P]
        flat = scr[:, 12:18, :].rearrange("p a n -> p (a n)")
        win = [flat[:, i * NPOOL * (T + 16):(i + 1) * NPOOL * (T + 16)].rearrange("p (g n) -> p g n", g=NPOOL)
               for i in range(2)]

        def mats(ap):
            return ap.rearrange("p (m n) -> p m n", m=4)

        def over(vec4):
            return vec4.unsqueeze(2).broadcast_to([P, 4, P])

        w_in = a["w_in"].rearrange("l (k p) n -> l p k n", p=P)
        w_up = a["ffn_w_up"].rearrange("l (k p) n -> l p k n", p=P)
        w_out = a["w_out"].rearrange("l (k p) n -> l p k n", p=P)
        w_down = a["ffn_w_down"].rearrange("l (k p) n -> l p k n", p=P)
        raw_a = raw[:, :, :].rearrange("p s (k n) -> p s k n", n=256)
        raw_b = raw[:, :, :].rearrange("p s (k n) -> p s k n", n=D)

        landed = [sem("landed0"), sem("landed1")]
        hi_done, lo_done, sub_used = sem("hi_done"), sem("lo_done"), sem("sub_used")

        def at(l):
            return bass.ds(l, 1)

        def hold(eng, s, value):
            eng.wait_ge(s, value)
            eng.sem_inc(sem("passed"), 1)

        blk = ctx.enter_context(nc.Block())

        A_PAIRS = N_IN + N_UP

        def sub_count(l, q, j=0):
            return l * SUBS + 8 * j + (4 * q + 8)

        def gates_act(act, l):
            act.wait_ge(sem("gate_x"), l + 1)
            act.activation(gtmp[:, 1], gtmp[:, 0], ACT.Abs).then_inc(sem("gate_abs"), 1)
            act.drain()
            act.activation(gtmp[:, 1], gtmp[:, 1], ACT.Exp, scale=-1.0)
            act.activation(gtmp[:, 2], ba[:, :, 0:DN_H].rearrange("p t h -> p h t"), ACT.Exp, scale=-1.0)
            act.activation(heads[:, 0, :], heads[:, 0, :], ACT.Exp)
            act.drain()
            act.activation(gtmp[:, 1], gtmp[:, 1], ACT.Ln, bias=1.0).then_inc(sem("gate_ln"), 1)
            act.wait_ge(sem("gate_sums"), l + 1)
            act.activation(gate[:, 3], gate[:, 1], ACT.Exp)
            act.activation(gate[:, 4], gtmp[:, 3], ACT.Exp)
            act.activation(gate[:, 5:7].rearrange("p v h t -> p (v h t)"), ps[:, 0, 24:48],
                           ACT.Exp).then_inc(sem("gate_exp"), 1)

        def swa_act(act, l):
            with act.Fori(0, SWA_KV) as kv:
                v = l * SWA_KV + kv + 1
                act.wait_ge(sem("swa_out"), v)
                act.activation(v_st, act_t[:, bass.ds(kv + T_SV, 1), :].rearrange("p a n -> p (a n)"),
                               ACT.Copy).then_inc(sem("v_staged"), 1)
                act.wait_ge(sem("v_turned"), v)
                act.activation(v_tok, ps[:, 0, 0:T], ACT.Copy).then_inc(sem("v_tok_ready"), 1)
                act.wait_ge(sem("max_ready"), v)
                for i in range(REP):
                    for b in range(2):
                        pr = prob[:, i, 0:P] if b == 0 else prob[:, i, P:3 * P]
                        act.activation(pr, pr, ACT.Exp, bias=soft[:, 1, i, b:b + 1],
                                       accum_out=soft[:, 3, i, b:b + 1])
                act.activation(soft[:, 2], soft[:, 2], ACT.Exp).then_inc(sem("exps_done"), 1)
                act.wait_ge(sem("p_turned"), v)
                for i in range(REP):
                    ins = act.activation(prob_t[:, i, :], ps[:, 4 + i, 0:3 * P], ACT.Copy)
                ins.then_inc(sem("prob_t_ready"), 1)

        def pool_act(act, l):
            act.wait_ge(sem("pool_mixed"), l + 1)
            for g in range(NPOOL):
                ins = act.activation(act_t[:, T_POOL + g, :], ps[:, 1 + g // 2, (g % 2) * T:(g % 2 + 1) * T],
                                     ACT.Copy, scale=par[:, R_PS + g:R_PS + g + 1])
            ins.then_inc(sem("pool_out"), 1)

        def delta_act(act, l):
            with act.Fori(0, NG) as g:
                v = l * NG + g + 1
                act.wait_ge(sem("delta_out"), v)
                for dst, t0 in ((q_s, T_QKV), (k_s, T_QKV + DN_H), (v_s, T_QKV + 2 * DN_H), (z_s, T_Z)):
                    act.activation(dst, act_t[:, bass.ds(2 * g + t0, 2), :].rearrange("p a n -> p (a n)"),
                                   ACT.Silu).then_inc(sem("dn_silued"), 1)
                act.wait_ge(sem("qkv_turned"), 3 * v - 1)
                act.activation(e1, ps[:, 2, :], ACT.Square)
                act.activation(e2, ps[:, 3, :], ACT.Square).then_inc(sem("qk_squared"), 1)
                for i, dst in enumerate((kn_t, qn_t, qd_t)):
                    act.wait_ge(sem("normed_turned"), 3 * v - 2 + i)
                    act.activation(dst, ps[:, 5 + i, :], ACT.Copy).then_inc(sem("normed_copied"), 1)
                act.wait_ge(sem("decay_arg"), v)
                act.activation(e1, e1, ACT.Exp, scale=-1.0)
                act.activation(e2, e2, ACT.Exp).then_inc(sem("decayed"), 1)
                act.wait_ge(sem("n_turned"), v)
                act.activation(pw_t, ps[:, 5, :], ACT.Copy).then_inc(sem("nt_copied"), 1)
                for k in range(5):
                    act.wait_ge(sem("squared"), 5 * v - 4 + k)
                    act.activation(pw, ps[:, 3, :], ACT.Copy).then_inc(sem("pw_copied"), 1)
                act.wait_ge(sem("uw_done"), v)
                act.activation(u_m, ps[:, 5, :], ACT.Copy).then_inc(sem("u_copied"), 1)
                act.wait_ge(sem("o_done"), v)
                act.activation(o_m, ps[:, 6, :], ACT.Copy)
                act.activation(e2, ps[:, 6, :], ACT.Square).then_inc(sem("o_squared"), 1)

        def gates_dve(dve, l):
            dve.drain()
            dve.tensor_tensor(gtmp[:, 0], ba[:, :, DN_H:NBA].rearrange("p t h -> p h t"),
                              heads[:, 1, :].unsqueeze(2).broadcast_to([P, DN_H, TT]), ALU.add)
            dve.drain().then_inc(sem("gate_x"), 1)
            dve.wait_ge(sem("gate_abs"), l + 1)
            dve.tensor_scalar(gtmp[:, 0], gtmp[:, 0], 0.0, None, ALU.max)
            dve.wait_ge(sem("gate_ln"), l + 1)
            dve.tensor_scalar(gtmp[:, 2], gtmp[:, 2], 1.0, None, ALU.add)
            dve.drain()
            dve.tensor_tensor(gtmp[:, 0], gtmp[:, 0], gtmp[:, 1], ALU.add)
            dve.reciprocal(gate[:, 2], gtmp[:, 2])
            dve.drain()
            dve.scalar_tensor_tensor(gate[:, 0], gtmp[:, 0], -1.0,
                                     heads[:, 0, :].unsqueeze(2).broadcast_to([P, DN_H, TT]), ALU.mult, ALU.mult)
            dve.drain().then_inc(sem("gate_g_ready"), 1)
            dve.wait_ge(sem("gate_summed"), l + 1)
            dve.tensor_copy(gate[:, 1].rearrange("p h t -> p (h t)"), ps[:, 0, 0:12])
            dve.drain()
            dve.tensor_tensor(gtmp[:, 3].rearrange("p h t -> p (h t)"), ps[:, 0, 12:24],
                              gate[:, 1].rearrange("p h t -> p (h t)"), ALU.subtract)
            dve.drain().then_inc(sem("gate_sums"), 1)

        def swa_dve(dve, l):
            with dve.Fori(0, SWA_KV) as kv:
                v = l * SWA_KV + kv + 1
                q3 = act_t[:, bass.ds(3 * kv + T_SQ, 3), :]
                k1 = act_t[:, bass.ds(kv + T_SK, 1), :]
                dve.drain()
                for src, c0, n in ((q3, 0, 3), (k1, 3, 1)):
                    for to, of in ((0, 64), (64, 0)):
                        dve.tensor_tensor(rope_x[to:to + 64, c0:c0 + n, :], src[of:of + 64],
                                          sin_t[of:of + 64, :].unsqueeze(1).broadcast_to([64, n, T]), ALU.mult)
                    dve.tensor_tensor(roped[:, c0:c0 + n, :], src, cos_t[:].unsqueeze(1).broadcast_to([P, n, T]),
                                      ALU.mult)
                dve.drain()
                dve.tensor_tensor(roped, roped, rope_x, ALU.add).then_inc(sem("roped"), 1)
                dve.wait_ge(sem("scores_done"), v)
                dve.scalar_tensor_tensor(prob, ps[:, 1:4, 0:3 * P], QSCALE,
                                         const[:, C_SWA:C_SWA + 3 * P].unsqueeze(1).broadcast_to([P, REP, 3 * P]),
                                         ALU.mult, ALU.add)
                dve.drain()
                dve.tensor_reduce(soft[:, 0, :, 0], prob[:, :, 0:P], AX.X, ALU.max)
                dve.tensor_reduce(soft[:, 0, :, 1], prob[:, :, P:3 * P], AX.X, ALU.max)
                dve.drain()
                sinks = heads[:, 2, bass.ds(3 * kv, 3)].unsqueeze(2).broadcast_to([P, REP, 2])
                dve.tensor_tensor(soft[:, 0], soft[:, 0], sinks, ALU.max)
                dve.drain()
                dve.tensor_scalar(soft[:, 1], soft[:, 0], -1.0, None, ALU.mult)
                dve.tensor_tensor(soft[:, 2], sinks, soft[:, 0], ALU.subtract)
                dve.drain().then_inc(sem("max_ready"), 1)
                dve.wait_ge(sem("exps_done"), v)
                dve.tensor_tensor(soft[:, 3], soft[:, 3], soft[:, 2], ALU.add)
                dve.drain()
                dve.reciprocal(soft[:, 3], soft[:, 3])
                dve.drain()
                for b, sl in ((0, slice(0, P)), (1, slice(P, 3 * P))):
                    n = P * (b + 1)
                    dve.tensor_tensor(prob[:, :, sl], prob[:, :, sl],
                                      soft[:, 3, :, b].unsqueeze(2).broadcast_to([P, REP, n]), ALU.mult)
                dve.drain().then_inc(sem("p_ready"), 1)
                dve.wait_ge(sem("pv_done"), v)
                dve.tensor_scalar(act_t[:, bass.ds(3 * kv + T_SQ, 2), :].rearrange("p a n -> p (a n)"), ps[:, 7, :],
                                  1.0, None, ALU.mult)
                dve.tensor_scalar(act_t[:, bass.ds(3 * kv + (T_SQ + 2), 1), :].rearrange("p a n -> p (a n)"),
                                  ps[:, 0, 0:T], 1.0, None, ALU.mult)
                dve.drain().then_inc(sem("swa_out"), 1)

        def pool_dve(dve, l):
            dve.memset(win[0][:, :, 0:16], 0.0)
            dve.memset(win[1][:, :, 0:16], 0.0)
            dve.tensor_copy(win[0][:, :, 16:], act_t[:, T_POOL:T_POOL + NPOOL, :])
            for i in range(NPOOL):
                s, d = win[i % 2], win[(i + 1) % 2]
                dve.drain()
                dve.tensor_tensor(d[:, i:, 16:], s[:, i:, 16:], s[:, i:, 16 - 2 ** i:16 + T - 2 ** i], ALU.add)
            dve.drain()
            for g in range(NPOOL):
                s = win[(g + 1) % 2][:, g, :]
                dve.tensor_tensor(s[:, 16:32], s[:, 16:32], const[:, C_COR + 16 * g:C_COR + 16 * (g + 1)], ALU.mult)
            dve.drain()
            for g in range(NPOOL):
                s = win[(g + 1) % 2][:, g, 16:]
                dve.scalar_tensor_tensor(s, s, 1.0 / WINDOWS[g], act_t[:, T_POOL + g, :], ALU.mult, ALU.subtract)
            dve.drain().then_inc(sem("pooled"), 1)
            hold(dve, sem("pool_mixed"), l + 1)

        def delta_dve(dve, l):
            hold(dve, sem("gate_exp"), l + 1)
            with dve.Fori(0, NG) as g:
                v = l * NG + g + 1
                dve.drain()
                dve.tensor_copy(gate_g[:], gate[:, :, bass.ds(2 * g, 2), :].rearrange("p v h t -> p v (h t)"))
                dve.drain()
                G, GC, BETA, EG, KD = (gate_g[:, i, :] for i in range(5))
                dve.wait_ge(sem("dn_silued"), 4 * v)
                dve.tensor_copy(mats(gb), over(G)).then_inc(sem("g_spread"), 1)
                dve.wait_ge(sem("qk_squared"), v)
                dve.tensor_reduce(vec[:, 0, :], mats(e1), AX.X, ALU.add)
                dve.tensor_reduce(vec[:, 1, :], mats(e2), AX.X, ALU.add)
                dve.tensor_tensor(vec[:, 6, :], BETA, EG, ALU.mult)
                dve.tensor_scalar(vec[:, 10, :], BETA, -1.0, None, ALU.mult)
                dve.drain()
                dve.tensor_scalar(vec[:, 0:2, :], vec[:, 0:2, :], EPS, None, ALU.add)
                dve.drain().then_inc(sem("qk_ms"), 1)
                dve.wait_ge(sem("qk_rs"), v)
                dve.tensor_tensor(mats(kn), mats(ps[:, 3, :]), over(vec[:, 3, :]), ALU.mult).then_inc(sem("normed"), 1)
                dve.tensor_scalar(vec[:, 4, :], vec[:, 2, :], QSCALE, None, ALU.mult)
                dve.tensor_tensor(vec[:, 6, :], vec[:, 6, :], vec[:, 3, :], ALU.mult)
                dve.tensor_tensor(vec[:, 7, :], KD, vec[:, 3, :], ALU.mult)
                dve.drain()
                dve.tensor_tensor(mats(qn), mats(ps[:, 2, :]), over(vec[:, 4, :]), ALU.mult).then_inc(sem("normed"), 1)
                dve.tensor_tensor(vec[:, 5, :], vec[:, 4, :], EG, ALU.mult)
                dve.drain()
                dve.tensor_tensor(mats(qd), mats(ps[:, 2, :]), over(vec[:, 5, :]), ALU.mult).then_inc(sem("normed"), 1)
                dve.tensor_tensor(mats(kbeg), mats(ps[:, 3, :]), over(vec[:, 6, :]), ALU.mult)
                dve.tensor_tensor(mats(kdec), mats(ps[:, 3, :]), over(vec[:, 7, :]), ALU.mult)
                dve.wait_ge(sem("qkv_turned"), 3 * v)
                dve.tensor_tensor(mats(vb), mats(ps[:, 4, :]), over(BETA), ALU.mult)
                dve.drain().then_inc(sem("scaled"), 1)
                dve.wait_ge(sem("gc_rows"), v)
                dve.tensor_tensor(mats(gb), mats(ps[:, 2, :]), over(GC), ALU.subtract)
                dve.drain()
                dve.tensor_scalar(e1, gb, 0.0, None, ALU.max)
                dve.tensor_scalar(e2, gb, 0.0, None, ALU.min)
                dve.drain().then_inc(sem("decay_arg"), 1)
                dve.wait_ge(sem("decayed"), v)
                for m in range(4):
                    em = mats(e1)[:, m, :]
                    dve.scalar_tensor_tensor(em, em, vec[:, 10, m:m + 1], lower, ALU.mult, ALU.mult)
                dve.tensor_tensor(mats(e2), mats(e2), upper.unsqueeze(1).broadcast_to([P, 4, P]), ALU.mult)
                dve.drain()
                dve.wait_ge(sem("kk_done"), v)
                dve.tensor_tensor(pw, ps[:, 3, :], e1, ALU.mult).then_inc(sem("n_ready"), 1)
                dve.wait_ge(sem("qk_done"), v)
                dve.tensor_tensor(attn, ps[:, 4, :], e2, ALU.mult).then_inc(sem("attn_ready"), 1)
                dve.wait_ge(sem("nt_copied"), v)
                dve.tensor_tensor(mats(inv), mats(pw_t), ident.unsqueeze(1).broadcast_to([P, 4, P]),
                                  ALU.add).then_inc(sem("inv_ready"), 1)
                for k in range(5):
                    if k < 4:
                        if k == 0:
                            dve.drain()
                        dve.wait_ge(sem("squared"), 5 * v - 4 + k)
                        dve.tensor_copy(pw_t, ps[:, 4, :]).then_inc(sem("pwt_copied"), 1)
                    dve.wait_ge(sem("inv_product"), 5 * v - 4 + k)
                    dve.tensor_tensor(inv, inv, ps[:, 6, :], ALU.add).then_inc(sem("inv_ready"), 1)
                dve.wait_ge(sem("uw_done"), v)
                dve.tensor_copy(w_t, ps[:, 7, :])
                dve.memset(state, 0.0)
                dve.drain().then_inc(sem("state_ready"), 1)
                dve.wait_ge(sem("u_copied"), v)
                for n in range(4):
                    t, c = n // 2, n % 2
                    r = slice(CH * c, CH * (c + 1))
                    dve.wait_ge(sem("ws_done"), 4 * v - 3 + n)
                    dve.tensor_tensor(v_new[r, :].rearrange("p (h n) -> p h n", h=2), mats(u_m)[r, t::2, :],
                                      ps[r, 2, 0:256].rearrange("p (h n) -> p h n", h=2),
                                      ALU.subtract).then_inc(sem("v_new_ready"), 1)
                    if n < 3:
                        dve.wait_ge(sem("state_add"), 3 * v - 2 + n)
                        for h in range(2):
                            sh = state[:, h * P:(h + 1) * P]
                            dve.scalar_tensor_tensor(sh, sh, gate_g[:, 5 + c, 2 * h + t:2 * h + t + 1],
                                                     ps[:, 3, h * P:(h + 1) * P], ALU.mult, ALU.add)
                        dve.drain().then_inc(sem("state_ready"), 1)
                dve.wait_ge(sem("o_squared"), v)
                dve.tensor_reduce(vec[:, 8, :], mats(e2), AX.X, ALU.add)
                dve.drain()
                dve.tensor_scalar(vec[:, 8, :], vec[:, 8, :], 1.0 / HD, EPS, ALU.mult, ALU.add)
                dve.drain().then_inc(sem("o_ms"), 1)
                dve.wait_ge(sem("o_rs"), v)
                dve.tensor_tensor(mats(o_m), mats(o_m), over(vec[:, 9, :]), ALU.mult).then_inc(sem("o_ready"), 1)
                dve.wait_ge(sem("o_turned"), v)
                dve.scalar_tensor_tensor(act_t[:, bass.ds(2 * g, 2), :].rearrange("p a n -> p (a n)"), ps[:, 4, :],
                                         par[:, R_DNW:R_DNW + 1], z_s, ALU.mult, ALU.mult)
                dve.drain().then_inc(sem("delta_out"), 1)

        def gates_pe(pe, l):
            pe.wait_ge(sem("gate_g_ready"), l + 1)
            gm = gate[:, 0].rearrange("p h t -> p (h t)")
            chunk0, chunk1 = (block[:, CH * c:CH * c + 1].broadcast_to([P, P]) for c in range(2))
            for i, w in enumerate((upper, block, chunk0, chunk1)):
                ins = pe.matmul(ps[:, 0, 12 * i:12 * (i + 1)], w, gm, start=True, stop=True)
            ins.then_inc(sem("gate_summed"), 1)

        def swa_pe(pe, l):
            hold(pe, sem("gate_exp"), l + 1)
            with pe.Fori(0, SWA_KV) as kv:
                v = l * SWA_KV + kv + 1
                pe.wait_ge(sem("swa_out"), v)
                pe.wait_ge(sem("v_staged"), v)
                for t in range(TT):
                    ins = pe.transpose(ps[:, 0, t * P:(t + 1) * P], v_st[:, t * P:(t + 1) * P], ident)
                ins.then_inc(sem("v_turned"), 1)
                pe.wait_ge(sem("roped"), v)
                for i in range(REP):
                    pe.matmul(ps[:, 1 + i, 0:P], roped[:, i, 0:P], roped[:, 3, 0:P], start=True, stop=True)
                    ins = pe.matmul(ps[:, 1 + i, P:3 * P], roped[:, i, P:T], roped[:, 3, :], start=True, stop=True)
                ins.then_inc(sem("scores_done"), 1)
                pe.wait_ge(sem("p_ready"), v)
                for i in range(REP):
                    for b in range(3):
                        ins = pe.transpose(ps[:, 4 + i, b * P:(b + 1) * P], prob[:, i, b * P:(b + 1) * P], ident)
                ins.then_inc(sem("p_turned"), 1)
                pe.wait_ge(sem("v_tok_ready"), v)
                pe.wait_ge(sem("prob_t_ready"), v)
                for i in range(REP):
                    bank, c = (7, i * T) if i < 2 else (0, 0)
                    pt = prob_t[:, i, :]
                    pe.matmul(ps[:, bank, c:c + P], v_tok[:, 0:P], pt[:, 0:P], start=i != 1, stop=True,
                              skip_group_check=True)
                    pe.matmul(ps[:, bank, c + P:c + T], v_tok[:, 0:P], pt[:, P:2 * P], start=False, stop=False,
                              skip_group_check=True)
                    ins = pe.matmul(ps[:, bank, c + P:c + T], v_tok[:, P:T], pt[:, 2 * P:3 * P], start=False,
                                    stop=True, skip_group_check=True)
                ins.then_inc(sem("pv_done"), 1)

        def pool_pe(pe, l):
            pe.wait_ge(sem("pooled"), l + 1)
            for g in range(NPOOL):
                ins = pe.matmul(ps[:, 1 + g // 2, (g % 2) * T:(g % 2 + 1) * T], pool_w[:, g, :],
                                win[(g + 1) % 2][:, g, 16:], start=True, stop=True)
            ins.then_inc(sem("pool_mixed"), 1)

        def delta_pe(pe, l):
            hold(pe, sem("pool_out"), l + 1)

            def four(bank, w, r):
                w, r = mats(w), mats(r)
                for m in range(4):
                    ins = pe.matmul(ps[:, bank, m * P:(m + 1) * P], w[:, m, :], r[:, m, :], start=True, stop=True)
                return ins

            def turn(bank, src):
                for m in range(4):
                    ins = pe.transpose(ps[:, bank, m * P:(m + 1) * P], mats(src)[:, m, :], ident)
                return ins

            with pe.Fori(0, NG) as g:
                v = l * NG + g + 1
                pe.wait_ge(sem("delta_out"), v)
                for i, src in enumerate((q_s, k_s, v_s)):
                    pe.wait_ge(sem("dn_silued"), 4 * v - 3 + i)
                    turn(2 + i, src).then_inc(sem("qkv_turned"), 1)
                for i, src in enumerate((kn, qn, qd)):
                    pe.wait_ge(sem("normed"), 3 * v - 2 + i)
                    turn(5 + i, src).then_inc(sem("normed_turned"), 1)
                pe.wait_ge(sem("g_spread"), v)
                pe.wait_ge(sem("scaled"), v)
                for m in range(4):
                    ins = pe.matmul(ps[:, 2, m * P:(m + 1) * P], mats(gb)[:, m, :], upper, start=True, stop=True)
                ins.then_inc(sem("gc_rows"), 1)
                pe.wait_ge(sem("normed_copied"), 3 * v - 1)
                four(3, kn_t, kn_t).then_inc(sem("kk_done"), 1)
                four(4, kn_t, qn_t).then_inc(sem("qk_done"), 1)
                pe.wait_ge(sem("n_ready"), v)
                turn(5, pw).then_inc(sem("n_turned"), 1)
                pe.wait_ge(sem("attn_ready"), v)
                for k in range(5):
                    if k == 0:
                        pe.wait_ge(sem("nt_copied"), v)
                    else:
                        pe.wait_ge(sem("pwt_copied"), 4 * v - 4 + k)
                    ins = four(3, pw_t, pw)
                    if k < 4:
                        ins = four(4, pw, pw_t)
                    ins.then_inc(sem("squared"), 1)
                    pe.wait_ge(sem("pw_copied"), 5 * v - 4 + k)
                    pe.wait_ge(sem("inv_ready"), 6 * v - 5 + k)
                    four(6, pw, inv).then_inc(sem("inv_product"), 1)
                pe.wait_ge(sem("inv_ready"), 6 * v)
                pe.wait_ge(sem("normed_copied"), 3 * v)
                four(5, inv, vb)
                four(7, kbeg, inv).then_inc(sem("uw_done"), 1)
                for n in range(4):
                    t, c = n // 2, n % 2
                    r = slice(CH * c, CH * (c + 1))
                    pe.wait_ge(sem("state_ready"), 4 * v - 3 + n)
                    for h in range(2):
                        m = 2 * h + t
                        cols = slice(m * P + CH * c, m * P + CH * (c + 1))
                        ins = pe.matmul(ps[r, 2, h * P:(h + 1) * P], w_t[:, cols], state[:, h * P:(h + 1) * P],
                                        start=True, stop=True)
                    ins.then_inc(sem("ws_done"), 1)
                    for h in range(2):
                        m = 2 * h + t
                        cols = slice(m * P + CH * c, m * P + CH * (c + 1))
                        pe.matmul(ps[r, 6, m * P:(m + 1) * P], qd_t[:, cols], state[:, h * P:(h + 1) * P],
                                  start=h == 0, stop=False, skip_group_check=True)
                    hold(pe, sem("v_new_ready"), 4 * v - 3 + n)
                    if n < 3:
                        for h in range(2):
                            m = 2 * h + t
                            ins = pe.matmul(ps[:, 3, h * P:(h + 1) * P], kdec[r, m * P:(m + 1) * P],
                                            v_new[r, h * P:(h + 1) * P], start=True, stop=True)
                        ins.then_inc(sem("state_add"), 1)
                    for h in range(2):
                        m = 2 * h + t
                        cols = slice(m * P + CH * c, m * P + CH * (c + 1))
                        ins = pe.matmul(ps[r, 6, m * P:(m + 1) * P], attn[r, cols], v_new[r, h * P:(h + 1) * P],
                                        start=False, stop=True, skip_group_check=True)
                    if n == 3:
                        ins.then_inc(sem("o_done"), 1)
                pe.wait_ge(sem("o_ready"), v)
                turn(4, o_m).then_inc(sem("o_turned"), 1)

        @blk.sync
        def _(sp):
            sp.dma_start(const[:], a["consts"]).then_inc(sem("const_in"), 16)
            sp.dma_start(scr[:, 0, 0:T].bitcast(I32),
                         a["positions"].broadcast_to([P, T])).then_inc(sem("pos_in"), 16)
            sp.dma_start(x[:], a["x"].rearrange("b (t p) d -> p (b t) d", p=P)).then_inc(sem("x_in"), 16)

            def pair(l, q, j, dst, src):
                sp.wait_ge(lo_done, l * SUBS + 8 * j + (4 * q + 4))
                sp.dma_start(dst, src).then_inc(landed[q % 2], 16)

            def form_a(l, q, j, w, col):
                pair(l, q, j, raw_a[:, q % 2, :, :],
                     w[at(l), :, :, bass.ds(col, 256)].rearrange("l p k n -> (l p) k n"))

            def form_b(l, q, j, w, k):
                pair(l, q, j, raw_b[:, q % 2, :, :],
                     w[at(l), :, bass.ds(k, 2), :].rearrange("l p k n -> (l p) k n"))

            def post_weights(l, name):
                sp.dma_start(w_post.rearrange("p a n -> p (a n)"),
                             a[name][at(l), :].broadcast_to([P, D])).then_inc(sem("post_w_in"), 16)

            with sp.Fori(0, DEPTH) as l:
                sp.wait_ge(sem("mixed"), l + 1)
                dnc = a["dn_conv_w"].rearrange("l k (r c) -> l (k r) c", c=P)
                loads = [(rows1[r:r + n, :], v[at(l), :, :].rearrange("l r c -> (l r) c")) for r, n, v in (
                    (R_PRE, KT, a["norm_mix_pre"].rearrange("l (r c) -> l r c", c=P)),
                    (R_FFN, KT, a["norm_ffn_pre"].rearrange("l (r c) -> l r c", c=P)),
                    (R_DNC, DN_TAPS * DN_TILES, dnc),
                    (R_PS, NPOOL, a["pool_scale"].rearrange("l (r c) -> l r c", c=P)),
                    (R_DNW, 1, a["dn_norm_w"].rearrange("l (r c) -> l r c", c=P)))]
                fc = a["ffn_conv_w"].rearrange("l k (r c) -> l (k r) c", c=P)
                fb = a["ffn_conv_b"].rearrange("l (r c) -> l r c", c=P)
                loads += [(rows2[p0:p0 + r1 - r0, b, :], src[at(l), r0:r1, :].rearrange("l r c -> (l r) c"))
                          for src, r0, r1, b, p0 in ((fc, 0, 128, 0, 0), (fc, 128, 256, 1, 0),
                                                     (fc, 256, 264, 2, 0), (fb, 0, 88, 2, 8))]
                loads += [(heads[:, i, :], a[name][at(l), :].broadcast_to([P, DN_H]))
                          for i, name in enumerate(("dn_a_log", "dn_dt_bias", "swa_sinks"))]
                loads.append((pool_w[:], a["pool_w"][at(l)].rearrange("l g c d -> (l c) g d")))
                assert len(loads) == N_PARAM_DMAS
                for dst, src in loads:
                    sp.dma_start(dst, src).then_inc(sem("params_in"), 16)

                with sp.Fori(0, 4) as j:
                    form_a(l, 0, j, w_in, 512 * j)
                    form_a(l, 1, j, w_in, 512 * j + 256)
                form_a(l, 8, 0, w_in, 2048)
                pair(l, GATE_PAIR, 0, raw[:, 1, 0:KT * NBA].rearrange("p (k n) -> p k n", n=NBA),
                     w_in[at(l), :, :, COL_BA:COL_BA + NBA].rearrange("l p k n -> (l p) k n"))
                for i, (col, _) in enumerate(TAIL):
                    form_a(l, 10 + i, 0, w_in, col)
                with sp.Fori(0, N_OUT // 2) as j:
                    form_b(l, P_OUT, j, w_out, 4 * j)
                    form_b(l, P_OUT + 1, j, w_out, 4 * j + 2)
                sp.wait_ge(sem("mixed"), l + 2)
                post_weights(l, "norm_mix_post")
                with sp.Fori(0, N_UP // 2) as j:
                    form_a(l, P_UP, j, w_up, 256 * j)
                    form_a(l, P_UP + 1, j, w_up, 256 * j + FF)
                sp.wait_ge(sem("x_new"), 4 * l + 6)
                post_weights(l, "norm_ffn_post")
                with sp.Fori(0, N_DOWN // 2) as j:
                    form_b(l, P_DOWN, j, w_down, 4 * j)
                    form_b(l, P_DOWN + 1, j, w_down, 4 * j + 2)
            sp.wait_ge(sem("x_new"), 4 * DEPTH + 4)
            sp.dma_start(out.rearrange("b (t p) d -> p (b t) d", p=P), x[:]).then_inc(sem("stored"), 16)
            sp.wait_ge(sem("stored"), 16)

        @blk.gpsimd
        def _(pool):
            pool.memset(mhalf[:], -0.5).then_inc(sem("mhalf_set"), 1)
            pool.wait_ge(sem("mhalf_set"), 1)

            def root(dst, src, n, of, value, done):
                pool.wait_ge(sem(of), value)
                pool.tensor_tensor(dst, src, mhalf[:, 0:n], ALU.pow).then_inc(sem(done), 1)

            def norm_roots(kind, l, f, s, d):
                for t in range(TT):
                    root(small[:, d + t:d + t + 1], small[:, s + t:s + t + 1], 1,
                         kind + "_ms", 4 * l + (2 * f + t + 1), kind + "_rs")

            with pool.Fori(0, DEPTH) as l:
                norm_roots("pre", l, 0, 24, 28)
                with pool.Fori(0, NG) as g:
                    root(vec[:, 2:4, :].rearrange("p a n -> p (a n)"), vec[:, 0:2, :].rearrange("p a n -> p (a n)"),
                         8, "qk_ms", l * NG + g + 1, "qk_rs")
                    root(vec[:, 9, :], vec[:, 8, :], 4, "o_ms", l * NG + g + 1, "o_rs")
                norm_roots("post", l, 0, 16, 20)
                norm_roots("pre", l, 1, 24, 28)
                norm_roots("post", l, 1, 16, 20)

        @blk.scalar
        def _(act):
            def hi(l, q, j=0, n=1024):
                act.wait_ge(landed[q % 2], l * (PAIRS // 2 * 16) + 16 * j + 16 * (q // 2 + 1))
                for s in range(4):
                    act.wait_ge(sub_used, l * SUBS + 8 * j + (4 * q + s + 1))
                    act.activation(w_hi[:, s, 0:n], raw[:, q % 2, s * n:(s + 1) * n], ACT.Copy).then_inc(hi_done, 1)

            def pre_norm(l, f, col):
                for t in range(TT):
                    act.wait_ge(sem("x_new"), 4 * l + (3 + 2 * f + t))
                    act.activation(h_tok[:, t, :], x[:, t, :], ACT.Square,
                                   accum_out=small[:, 22 + t:23 + t]).then_inc(sem("pre_ssq"), 1)
                for b in range(8):
                    act.wait_ge(sem("h_turned"), 16 * l + (8 * f + b + 1))
                    for i in range(2):
                        k = 2 * b + i
                        ins = act.activation(h_hi[:, k, :], ps[:, b, i * T:(i + 1) * T], ACT.Copy,
                                             scale=par[:, col + k:col + k + 1])
                    ins.then_inc(sem("h_hi_done"), 1)

            def post_norm(l, q_last):
                act.wait_ge(sub_used, sub_count(l, q_last))
                for t in range(TT):
                    for c in range(4):
                        ins = act.activation(h_tok[:, t, c * 512:(c + 1) * 512], ps[:, 4 * t + c, :], ACT.Square,
                                             accum_out=small[:, 4 * t + c:4 * t + c + 1])
                    ins.then_inc(sem("post_ssq"), 1)

            def x_hi(l, q, j, k, first=False):
                act.wait_ge(sub_used, l * SUBS + 8 * j + 4 * (first if first else q))
                act.activation(h_hi[:, 2 * (q % 2):2 * (q % 2) + 2, :], act_t[:, bass.ds(k, 2), :],
                               ACT.Copy).then_inc(sem("x_hi_done"), 1)

            def form_b(l, base, n):
                x_hi(l, base, 0, 0, base + 1)
                x_hi(l, base + 1, 0, 2, base + 1)
                hi(l, base + 1)
                with act.Fori(0, n // 2 - 1) as j:
                    for i in range(2):
                        x_hi(l, base + 2 + i, j, 4 * j + (4 + 2 * i))
                        hi(l, base + 2 + i, j)

            act.wait_ge(sem("angle_ready"), 1)
            act.activation(sin_t[:], scr[:, 1, 0:T], ACT.Sin).then_inc(sem("sined"), 1)
            act.activation(cos_t[:], scr[:, 1, 0:T], ACT.Sin, scale=0.5).then_inc(sem("sined"), 1)

            with act.Fori(0, DEPTH) as l:
                hi(l, 0)
                pre_norm(l, 0, R_PRE)
                hi(l, 1)

                def conv_init(l, q, j):
                    act.wait_ge(sub_used, sub_count(l, q, j))
                    for i in range(2):
                        tile = 4 * j + (2 * q + i)
                        ins = act.activation(act_t[:, bass.ds(tile + T_QKV, 1), :].rearrange("p a n -> p (a n)"),
                                             ps[:, q % 2, i * T:(i + 1) * T], ACT.Copy,
                                             scale=par[:, bass.ds(tile + (R_DNC + 3 * DN_TILES), 1)])
                    ins.then_inc(sem("conv_init"), 1)

                with act.Fori(0, 3) as j:
                    conv_init(l, 0, j)
                    hi(l, 2, j)
                    conv_init(l, 1, j)
                    hi(l, 3, j)
                conv_init(l, 6, 0)
                hi(l, 8)
                conv_init(l, 7, 0)
                hi(l, GATE_PAIR, 0, KT * NBA // 4)
                conv_init(l, 8, 0)
                with act.Fori(0, 5) as j:
                    hi(l, 10, j)
                    hi(l, 11, j)
                hi(l, P_OUT)
                gates_act(act, l)
                swa_act(act, l)
                pool_act(act, l)
                delta_act(act, l)
                act.wait_ge(sem("mixed"), l + 2)
                form_b(l, P_OUT, N_OUT)
                post_norm(l, P_OUT + N_OUT - 1)
                hi(l, P_UP)
                pre_norm(l, 1, R_FFN)
                hi(l, P_UP + 1)

                def ffn_init(l, j, ab):
                    act.wait_ge(sub_used, sub_count(l, P_UP + ab, j))
                    if ab == 0:
                        act.wait_ge(sem("hidden"), l * (FT // 2) + j + 1)
                    for i in range(2):
                        ins = act.activation(y_ab[:, ab, i, :], ps[:, ab, i * T:(i + 1) * T], ACT.Identity,
                                             scale=par[:, bass.ds(2 * j + (R_FC + 2 * 2 * FT + ab * FT + i), 1)],
                                             bias=par[:, bass.ds(2 * j + (R_FB + ab * FT + i), 1)])
                    ins.then_inc(sem("ffn_init"), 1)

                def silu(l, j):
                    act.wait_ge(sem("evacuated"), l * A_PAIRS + 2 * j + (N_IN + 1 + 2))
                    act.activation(y_ab[:, 0, :, :], y_ab[:, 0, :, :], ACT.Silu).then_inc(sem("silued"), 1)

                def up_step(l, j, last):
                    ffn_init(l, j, 0)
                    if not last:
                        hi(l, P_UP + 2, j)
                    silu(l, j)
                    ffn_init(l, j, 1)
                    if not last:
                        hi(l, P_UP + 3, j)

                with act.Fori(0, N_UP // 2 - 1) as j:
                    up_step(l, j, False)
                up_step(l, N_UP // 2 - 1, True)
                hi(l, P_DOWN)
                act.wait_ge(sem("hidden"), l * (FT // 2) + (FT // 2 + 1))
                form_b(l, P_DOWN, N_DOWN)
                post_norm(l, P_DOWN + N_DOWN - 1)

        @blk.vector
        def _(dve):
            def lo(l, q, j=0, n=1024):
                for s in range(4):
                    dve.wait_ge(hi_done, l * SUBS + 8 * j + (4 * q + s + 1))
                    dve.tensor_tensor(w_lo[:, s, 0:n], raw[:, q % 2, s * n:(s + 1) * n],
                                      w_hi[:, s, 0:n].bitcast(F32), ALU.subtract).then_inc(lo_done, 1)

            def mean(kind, l, f, n, ssq, ms):
                for t in range(TT):
                    dve.wait_ge(sem(kind + "_ssq"), 4 * l + (2 * f + t + 1))
                    if n > 1:
                        dve.tensor_reduce(small[:, 32 + t:33 + t], small[:, ssq + n * t:ssq + n * t + n], AX.X, ALU.add)
                        dve.drain()
                        src = small[:, 32 + t:33 + t]
                    else:
                        src = small[:, ssq + t:ssq + t + 1]
                    dve.tensor_scalar(small[:, ms + t:ms + t + 1], src, 1.0 / D, EPS, ALU.mult,
                                      ALU.add).then_inc(sem(kind + "_ms"), 1)
                    yield t

            def pre_norm(l, f, col):
                for t in mean("pre", l, f, 1, 22, 24):
                    dve.wait_ge(sem("pre_rs"), 4 * l + (2 * f + t + 1))
                    dve.tensor_scalar(h_tok[:, t, :], x[:, t, :], small[:, 28 + t:29 + t], None,
                                      ALU.mult).then_inc(sem("h_ready"), 1)
                for b in range(8):
                    dve.wait_ge(sem("h_hi_done"), 16 * l + (8 * f + b + 1))
                    for i in range(2):
                        k = 2 * b + i
                        ins = dve.scalar_tensor_tensor(h_lo[:, k, :], ps[:, b, i * T:(i + 1) * T],
                                                       par[:, col + k:col + k + 1], h_hi[:, k, :].bitcast(F32),
                                                       ALU.mult, ALU.subtract)
                    ins.then_inc(sem("h_lo_done"), 1)

            def post_norm(l, f):
                for t in mean("post", l, f, 4, 0, 16):
                    dve.wait_ge(sem("post_rs"), 4 * l + (2 * f + t + 1))
                    if t == 0:
                        dve.wait_ge(sem("post_w_in"), 32 * l + 16 * (f + 1))
                    for c in range(4):
                        dve.scalar_tensor_tensor(h_tok[:, t, c * 512:(c + 1) * 512], ps[:, 4 * t + c, :],
                                                 small[:, 20 + t:21 + t], w_post[:, c, :], ALU.mult, ALU.mult)
                    dve.drain()
                    dve.tensor_tensor(x[:, t, :], x[:, t, :], h_tok[:, t, :], ALU.add).then_inc(sem("x_new"), 1)

            def x_lo(l, q, j, k, f, m):
                dve.wait_ge(sem("x_hi_done"), l * (N_OUT + N_DOWN) + f * N_OUT + 2 * j + (m + 1))
                sl = slice(2 * (q % 2), 2 * (q % 2) + 2)
                dve.tensor_tensor(h_lo[:, sl, :], act_t[:, bass.ds(k, 2), :], h_hi[:, sl, :].bitcast(F32),
                                  ALU.subtract).then_inc(sem("x_lo_done"), 1)

            def form_b(l, base, n, f):
                x_lo(l, base, 0, 0, f, 0)
                x_lo(l, base + 1, 0, 2, f, 1)
                lo(l, base + 1)
                with dve.Fori(0, n // 2 - 1) as j:
                    for i in range(2):
                        x_lo(l, base + 2 + i, j, 4 * j + (4 + 2 * i), f, 2 + i)
                        lo(l, base + 2 + i, j)

            dve.memset(small[:], 0.0)
            dve.drain().then_inc(lo_done, 8)
            for name, n in (("evacuated", 2), ("mixed", 1), ("hidden", 1), ("swa_out", 1), ("delta_out", 1)):
                dve.drain().then_inc(sem(name), n)

            dve.wait_ge(sem("const_in"), 16)
            dve.wait_ge(sem("pos_in"), 16)
            pos, ang, turns = scr[:, 2, 0:T], scr[:, 1, 0:T], scr[:, 3, 0:T]
            dve.tensor_copy(pos, scr[:, 0, 0:T].bitcast(I32))
            dve.drain()
            dve.tensor_scalar(ang, pos, const[:, C_INVF:C_INVF + 1], None, ALU.mult)
            dve.drain()
            dve.tensor_scalar(turns, ang, 1.0 / (2 * np.pi), MAGIC, ALU.mult, ALU.add)
            dve.drain()
            dve.tensor_scalar(turns, turns, MAGIC, None, ALU.subtract)
            dve.drain()
            for part in TWO_PI:
                dve.scalar_tensor_tensor(ang, turns, -part, ang, ALU.mult, ALU.add)
                dve.drain()
            dve.tensor_scalar(ang, ang, PI_IN, -PI_IN, ALU.min, ALU.max).then_inc(sem("angle_ready"), 1)
            dve.wait_ge(sem("sined"), 2)
            dve.tensor_scalar(sin_t[:], sin_t[:], const[:, C_SGN:C_SGN + 1], None, ALU.mult)
            dve.tensor_tensor(cos_t[:], cos_t[:], cos_t[:], ALU.mult)
            dve.drain()
            dve.tensor_scalar(cos_t[:], cos_t[:], -2.0, 1.0, ALU.mult, ALU.add)
            dve.wait_ge(sem("x_in"), 16)
            dve.drain().then_inc(sem("x_new"), 4)

            with dve.Fori(0, DEPTH) as l:
                dve.wait_ge(sem("params_turned"), l + 1)
                dve.tensor_copy(par[:, 0:R_ONE], ps[:, 0, 0:R_ONE])
                dve.tensor_copy(par[:, R_ONE:R_ALL], ps[:, 1, 0:FROWS])
                dve.drain().then_inc(sem("par_ready"), 1)
                lo(l, 0)
                pre_norm(l, 0, R_PRE)
                lo(l, 1)

                def conv_taps(l, q, j):
                    dve.wait_ge(sem("conv_init"), l * 9 + 2 * j + (q + 1))
                    for k in range(1, DN_TAPS):
                        if k > 1:
                            dve.drain()
                        for i in range(2):
                            tile = 4 * j + (2 * q + i)
                            y = act_t[:, bass.ds(tile + T_QKV, 1), k:T].rearrange("p a n -> p (a n)")
                            ins = dve.scalar_tensor_tensor(
                                y, ps[:, q % 2, i * T:(i + 1) * T - k],
                                par[:, bass.ds(tile + (R_DNC + (3 - k) * DN_TILES), 1)], y, ALU.mult, ALU.add)
                    ins.then_inc(sem("evacuated"), 1)

                with dve.Fori(0, 3) as j:
                    conv_taps(l, 0, j)
                    lo(l, 2, j)
                    conv_taps(l, 1, j)
                    lo(l, 3, j)
                conv_taps(l, 6, 0)
                lo(l, 8)
                conv_taps(l, 7, 0)
                lo(l, GATE_PAIR, 0, KT * NBA // 4)
                conv_taps(l, 8, 0)
                lo(l, 10)
                dve.wait_ge(sub_used, sub_count(l, GATE_PAIR))
                dve.tensor_copy(ba[:].rearrange("p t n -> p (t n)"), ps[:, 1, 0:2 * NBA]).then_inc(sem("evacuated"), 1)
                for i, (_, tile) in enumerate(TAIL):
                    if i < 9:
                        lo(l, 11 + i)
                    dve.wait_ge(sub_used, sub_count(l, 10 + i))
                    dve.tensor_copy(act_t[:, tile:tile + 2, :].rearrange("p a n -> p (a n)"),
                                    ps[:, i % 2, :]).then_inc(sem("evacuated"), 1)
                lo(l, P_OUT)
                gates_dve(dve, l)
                swa_dve(dve, l)
                pool_dve(dve, l)
                delta_dve(dve, l)
                hold(dve, sem("pool_out"), l + 1)
                dve.drain().then_inc(sem("mixed"), 1)

                form_b(l, P_OUT, N_OUT, 0)
                post_norm(l, 0)
                lo(l, P_UP)
                pre_norm(l, 1, R_FFN)
                lo(l, P_UP + 1)

                def taps(l, j, ab):
                    dve.wait_ge(sem("ffn_init"), l * N_UP + 2 * j + (ab + 1))
                    for k in range(1, FFN_TAPS):
                        if k > 1:
                            dve.drain()
                        for i in range(2):
                            y = y_ab[:, ab, i, k:T]
                            ins = dve.scalar_tensor_tensor(
                                y, ps[:, ab, i * T:(i + 1) * T - k],
                                par[:, bass.ds(2 * j + (R_FC + (2 - k) * 2 * FT + ab * FT + i), 1)], y,
                                ALU.mult, ALU.add)
                    ins.then_inc(sem("evacuated"), 1)

                def up_step(l, j, last):
                    taps(l, j, 0)
                    if not last:
                        lo(l, P_UP + 2, j)
                    taps(l, j, 1)
                    dve.drain()
                    dve.wait_ge(sem("silued"), l * (FT // 2) + j + 1)
                    dve.tensor_tensor(act_t[:, bass.ds(2 * j, 2), :], y_ab[:, 0, :, :], y_ab[:, 1, :, :],
                                      ALU.mult).then_inc(sem("hidden"), 1)
                    if not last:
                        lo(l, P_UP + 3, j)

                with dve.Fori(0, N_UP // 2 - 1) as j:
                    up_step(l, j, False)
                up_step(l, N_UP // 2 - 1, True)
                lo(l, P_DOWN)
                dve.drain()
                form_b(l, P_DOWN, N_DOWN, 1)
                post_norm(l, 1)

        @blk.tensor
        def _(pe):
            def three(dst, w, wl, xs, xl, start):
                pe.matmul(dst, w, xs, start=start, stop=False, skip_group_check=True)
                pe.matmul(dst, w, xl, start=False, stop=False, skip_group_check=True)
                return pe.matmul(dst, wl, xs, start=False, stop=True, skip_group_check=True)

            def pair_a(l, q, j, n):
                pe.wait_ge(sem("evacuated"), l * A_PAIRS + 2 * j + (n + 1))
                for s in range(4):
                    pe.wait_ge(lo_done, l * SUBS + 8 * j + (4 * q + s + 9))
                    for i in range(2):
                        for kk in range(4):
                            k, c = 4 * s + kk, 256 * kk + 128 * i
                            ins = three(ps[:, q % 2, i * T:(i + 1) * T], w_hi[:, s, c:c + P], w_lo[:, s, c:c + P],
                                        h_hi[:, k, :], h_lo[:, k, :], k == 0 and i == 0)
                    ins.then_inc(sub_used, 1)

            def gate_pair(l):
                pe.wait_ge(sem("evacuated"), l * A_PAIRS + (GATE_PAIR + 1))
                for s in range(4):
                    pe.wait_ge(lo_done, l * SUBS + (4 * GATE_PAIR + s + 9))
                    for t in range(TT):
                        for kk in range(4):
                            k, c = 4 * s + kk, NBA * kk
                            dst, tok = ps[:, 1, t * NBA:(t + 1) * NBA], slice(t * P, (t + 1) * P)
                            ins = three(dst, h_hi[:, k, tok], h_lo[:, k, tok], w_hi[:, s, c:c + NBA],
                                        w_lo[:, s, c:c + NBA], k == 0 and t == 0)
                    ins.then_inc(sub_used, 1)

            def pair_b(l, q, j, m, f, first, last):
                pe.wait_ge(sem("x_lo_done"), l * (N_OUT + N_DOWN) + f * N_OUT + 2 * j + (m + 1))
                for s in range(4):
                    pe.wait_ge(lo_done, l * SUBS + 8 * j + (4 * q + s + 9))
                    k = 2 * (q % 2) + s // 2
                    for t in range(TT):
                        tok = slice(t * P, (t + 1) * P)
                        for c in range(2):
                            dst = ps[:, 4 * t + 2 * (s % 2) + c, :]
                            w, wl = (v[:, s, 512 * c:512 * (c + 1)] for v in (w_hi, w_lo))
                            ins = three(dst, h_hi[:, k, tok], h_lo[:, k, tok], w, wl, first and s < 2)
                    ins.then_inc(sub_used, 1)

            def form_b(l, base, n, f):
                for i in range(2):
                    pair_b(l, base + i, 0, i, f, i == 0, False)
                with pe.Fori(0, n // 2 - 1) as j:
                    for i in range(2):
                        pair_b(l, base + 2 + i, j, 2 + i, f, False, False)

            def pre_norm(l, f):
                pe.wait_ge(sem("h_ready"), 4 * l + (2 * f + 2))
                for b in range(8):
                    for i in range(2):
                        for t in range(TT):
                            k = 2 * b + i
                            ins = pe.transpose(ps[:, b, i * T + t * P:i * T + (t + 1) * P],
                                               h_tok[:, t, k * P:(k + 1) * P], ident)
                    ins.then_inc(sem("h_turned"), 1)
                hold(pe, sem("h_lo_done"), 16 * l + (8 * f + 8))

            pe.nop().then_inc(sub_used, 4)
            pe.wait_ge(sem("const_in"), 16)
            with pe.Fori(0, DEPTH) as l:
                pe.wait_ge(sem("params_in"), l * (16 * N_PARAM_DMAS) + 16 * N_PARAM_DMAS)
                pe.wait_ge(sem("x_new"), 4 * l + 4)
                pe.transpose(ps[:, 0, 0:R_ONE], rows1[0:R_ONE, :], ident[0:R_ONE, 0:R_ONE])
                for b, n in ((0, P), (1, P), (2, FROWS - 2 * P)):
                    ins = pe.transpose(ps[:, 1, b * P:b * P + n], rows2[0:n, b, :], ident[0:n, 0:n])
                ins.then_inc(sem("params_turned"), 1)
                pe.wait_ge(sem("par_ready"), l + 1)
                pre_norm(l, 0)
                with pe.Fori(0, 4) as j:
                    pair_a(l, 0, j, 0)
                    pair_a(l, 1, j, 1)
                pair_a(l, 8, 0, 8)
                gate_pair(l)
                with pe.Fori(0, 5) as j:
                    pair_a(l, 10, j, 10)
                    pair_a(l, 11, j, 11)
                pe.wait_ge(sem("evacuated"), l * A_PAIRS + (N_IN + 2))
                gates_pe(pe, l)
                swa_pe(pe, l)
                pool_pe(pe, l)
                delta_pe(pe, l)
                pe.wait_ge(sem("mixed"), l + 2)
                form_b(l, P_OUT, N_OUT, 0)
                pre_norm(l, 1)
                with pe.Fori(0, N_UP // 2) as j:
                    pair_a(l, P_UP, j, N_IN)
                    pair_a(l, P_UP + 1, j, N_IN + 1)
                pe.wait_ge(sem("evacuated"), l * A_PAIRS + (N_IN + N_UP + 2))
                form_b(l, P_DOWN, N_DOWN, 1)

N_PARAM_DMAS = 13
TWO_PI = (6.28125, 0.0019354820251464844, -1.7484555314695172e-07)
PI_IN = 3.1415925

_INS = ["x", "positions", "norm_mix_pre", "w_in", "dn_conv_w", "dn_a_log", "dn_dt_bias", "dn_norm_w", "pool_w",
        "pool_scale", "swa_sinks", "w_out", "norm_mix_post", "norm_ffn_pre", "ffn_w_up", "ffn_conv_w",
        "ffn_conv_b", "ffn_w_down", "norm_ffn_post"]


def kernel(**inputs):
    import concourse.bacc as bacc
    from concourse.bass_utils import run_bass_kernel_spmd

    nc = bacc.Bacc("TRN2", target_bir_lowering=False, num_devices=1)
    arrays, aps = {}, {}
    for name in _INS:
        v = np.ascontiguousarray(inputs[name])
        arrays["in_" + name] = v
        aps[name] = nc.dram_tensor("in_" + name, v.shape, mybir.dt.from_np(v.dtype), kind="ExternalInput").ap()
    arrays["in_consts"] = constants()
    aps["consts"] = nc.dram_tensor("in_consts", (P, C_ALL), F32, kind="ExternalInput").ap()
    out = nc.dram_tensor("out_x", (1, T, D), F32, kind="ExternalOutput").ap()
    trunk(nc, aps, out)
    r = run_bass_kernel_spmd(nc, [arrays], core_ids=[0])
    return r.results[0]["out_x"]
```

```python
from contextlib import ExitStack

import concourse.bass as bass
import numpy as np
from concourse import mybir

F32 = mybir.dt.float32
F32R = mybir.dt.float32r
I32 = mybir.dt.int32
ALU = mybir.AluOpType
ACT = mybir.ActivationFunctionType
AX = mybir.AxisListType

P = 128
D = 2048
T = 256
TT = T // P
KT = D // P
DEPTH = 2
HD = 128
DN_H = 6
DN_TILES = 3 * DN_H
DN_TAPS = 4
CH = 64
NG = 3
WINDOWS = (2, 4, 8, 16)
NPOOL = 4
SWA_H, SWA_KV = 6, 2
REP = SWA_H // SWA_KV
FF = 5632
FT = FF // P
FFN_TAPS = 3
EPS = 1e-6
QSCALE = HD ** -0.5
MAGIC = 12582912.0

COL_Z = 3 * DN_H * HD
COL_BA = COL_Z + DN_H * HD
COL_POOL = COL_BA + 2 * DN_H
COL_SQ = COL_POOL + NPOOL * P
COL_SK = COL_SQ + SWA_H * HD
COL_SV = COL_SK + SWA_KV * HD
NBA = 2 * DN_H

N_IN, N_OUT, N_UP, N_DOWN = 20, KT // 2, 2 * FT // 2, FT // 2
P_IN, P_OUT, P_UP, P_DOWN = 0, N_IN, N_IN + N_OUT, N_IN + N_OUT + N_UP
PAIRS = P_DOWN + N_DOWN
SUBS = 4 * PAIRS
HEAD = [(COL_SK, 40), (COL_SV, 42), (COL_SQ, 10), (COL_SQ + 256, 12), (COL_SQ + 512, 14)]
P_GROUP, P_POOL = 6, 18
T_POOL, T_SQ, T_QKV, T_Z, T_SK, T_SV = 6, 10, 16, 34, 40, 42

R_PRE, R_FFN, R_DNC, R_PS = 0, KT, 2 * KT, 2 * KT + DN_TAPS * DN_TILES
R_DNW = R_PS + NPOOL
R_ONE = R_DNW + 1
R_FC = R_ONE
R_FB = R_FC + FFN_TAPS * 2 * FT
R_ALL = R_FB + 2 * FT
FROWS = R_ALL - R_ONE

C_ID, C_U, C_LS, C_BD = 0, P, 2 * P, 3 * P
C_SWA = 4 * P
C_COR = C_SWA + 3 * P
C_INVF = C_COR + NPOOL * 16
C_SGN = C_INVF + 1
C_ALL = C_SGN + 1


def constants():
    c = np.zeros((P, C_ALL), np.float32)
    i, j = np.arange(P)[:, None], np.arange(P)[None, :]
    same = (i // CH) == (j // CH)
    c[:, C_ID:C_ID + P] = i == j
    c[:, C_U:C_U + P] = same & (i <= j)
    c[:, C_LS:C_LS + P] = same & (i > j)
    c[:, C_BD:C_BD + P] = same
    far = np.float32(-1e30)
    c[:, C_SWA:C_SWA + P] = np.where(j <= i, 0, far)
    c[:, C_SWA + P:C_SWA + 2 * P] = np.where(j > i, 0, far)
    c[:, C_SWA + 2 * P:C_SWA + 3 * P] = np.where(j <= i, 0, far)
    for g, w in enumerate(WINDOWS):
        c[:, C_COR + 16 * g:C_COR + 16 * (g + 1)] = w / np.minimum(np.arange(16) + 1, w)
    freq = (1.0 / np.float32(10000.0) ** (np.arange(0, HD, 2, dtype=np.float32) / np.float32(HD))).astype(np.float32)
    c[:, C_INVF] = np.concatenate([freq, freq])
    c[:, C_SGN] = np.where(np.arange(P) < HD // 2, 1, -1)
    return c


def trunk(nc, a, out):
    with ExitStack() as ctx:
        def sb(name, shape, dt=F32):
            return ctx.enter_context(nc.sbuf_tensor(name, shape, dt))

        used = {}

        def sem(name):
            if name not in used:
                used[name] = ctx.enter_context(nc.semaphore(name))
            return used[name]

        x = sb("x", [P, TT, D])
        h_hi = sb("h_hi", [P, KT, T], F32R)
        h_lo = sb("h_lo", [P, KT, T], F32R)
        raw = sb("raw", [P, 2, 4096])
        w_hi = sb("w_hi", [P, 4, 1024], F32R)
        w_lo = sb("w_lo", [P, 4, 1024], F32R)
        act_t = sb("act_t", [P, FT, T])
        scr = sb("scratch", [P, 18, 512])
        const = sb("const", [P, C_ALL])
        cos_t = sb("cos_t", [P, T])
        sin_t = sb("sin_t", [P, T])
        rows1 = sb("rows1", [P, P])
        rows2 = sb("rows2", [P, 3, P])
        par = sb("par", [P, R_ALL])
        pool_w = sb("pool_w", [P, NPOOL, P])
        heads = sb("heads", [P, 3, DN_H])
        small = sb("small", [P, 64])
        gate = sb("gate", [P, 7, DN_H, TT])
        gate_g = sb("gate_g", [P, 7, 4])
        gtmp = sb("gtmp", [P, 4, DN_H, TT])
        ba = sb("ba", [P, TT, NBA])
        vec = sb("vec", [P, 11, 4])
        soft = sb("soft", [P, 4, REP, 2])
        mhalf = sb("mhalf", [P, 16])
        ps = ctx.enter_context(nc.psum_tensor("ps", [P, 8, 512], F32))

        ident = const[:, C_ID:C_ID + P]
        upper = const[:, C_U:C_U + P]
        lower = const[:, C_LS:C_LS + P]
        block = const[:, C_BD:C_BD + P]

        h_tok = scr[:, 0:8, :].rearrange("p a (b n) -> p (a b n)", b=1).rearrange("p (t d) -> p t d", t=TT)
        w_post = scr[:, 8:12, :]
        y_ab = scr[:, 16:18, :].rearrange("p a (b n) -> p a b n", b=2)
        (q_s, k_s, v_s, z_s, qn, qd, kn, kbeg, kdec, vb, kn_t, qn_t, qd_t, e1, e2, vs, gb) = (
            scr[:, i, :] for i in range(17))
        pw, pw_t, inv, attn, u_m, w_t, o_m = q_s, k_s, v_s, qn, qd, kn, e1
        v_new, state = vs[:, 0:256], vs[:, 256:512]
        rope_x, roped = scr[:, 0:2, :].rearrange("p a (b n) -> p (a b) n", n=T), scr[:, 2:4, :].rearrange("p a (b n) -> p (a b) n", n=T)
        v_st, v_tok = scr[:, 4, 0:T], scr[:, 5, 0:T]
        prob, prob_t = scr[:, 6:9, 0:3 * P], scr[:, 9:12, 0:3 * P]
        flat = act_t[:, T_QKV:T_Z, :].rearrange("p a n -> p (a n)")
        win = [flat[:, i * NPOOL * (T + 16):(i + 1) * NPOOL * (T + 16)].rearrange("p (g n) -> p g n", g=NPOOL)
               for i in range(2)]

        def mats(ap):
            return ap.rearrange("p (m n) -> p m n", m=4)

        def over(vec4):
            return vec4.unsqueeze(2).broadcast_to([P, 4, P])

        w_in = a["w_in"].rearrange("l (k p) n -> l p k n", p=P)
        w_up = a["ffn_w_up"].rearrange("l (k p) n -> l p k n", p=P)
        w_out = a["w_out"].rearrange("l (k p) n -> l p k n", p=P)
        w_down = a["ffn_w_down"].rearrange("l (k p) n -> l p k n", p=P)
        raw_a = raw[:, :, :].rearrange("p s (k n) -> p s k n", n=256)
        raw_b = raw[:, :, :].rearrange("p s (k n) -> p s k n", n=D)

        landed = [sem("landed0"), sem("landed1")]
        hi_done, lo_done, sub_used = sem("hi_done"), sem("lo_done"), sem("sub_used")

        def at(l):
            return bass.ds(l, 1)

        def hold(eng, s, value):
            eng.wait_ge(s, value)
            eng.sem_inc(sem("passed"), 1)

        blk = ctx.enter_context(nc.Block())

        A_PAIRS = N_IN + N_UP

        def sub_count(l, q, j=0):
            return l * SUBS + 8 * j + (4 * q + 8)

        def gates_act(act, l):
            act.wait_ge(sem("gate_x"), l + 1)
            act.activation(gtmp[:, 1], gtmp[:, 0], ACT.Abs).then_inc(sem("gate_abs"), 1)
            act.drain()
            act.activation(gtmp[:, 1], gtmp[:, 1], ACT.Exp, scale=-1.0)
            act.activation(gtmp[:, 2], ba[:, :, 0:DN_H].rearrange("p t h -> p h t"), ACT.Exp, scale=-1.0)
            act.activation(heads[:, 0, :], heads[:, 0, :], ACT.Exp)
            act.drain()
            act.activation(gtmp[:, 1], gtmp[:, 1], ACT.Ln, bias=1.0).then_inc(sem("gate_ln"), 1)

        def decays_act(act, l):
            act.wait_ge(sem("gate_sums"), l + 1)
            act.activation(gate[:, 3], gate[:, 1], ACT.Exp)
            act.activation(gate[:, 4], gtmp[:, 3], ACT.Exp)
            act.activation(gate[:, 5:7].rearrange("p v h t -> p (v h t)"), ps[:, 2, 24:48],
                           ACT.Exp).then_inc(sem("gate_exp"), 1)

        def swa_act(act, l, kv, more, init):
            v = l * SWA_KV + kv + 1
            act.wait_ge(sem("swa_out"), v)
            act.wait_ge(sem("evacuated"), l * A_PAIRS + 8)
            act.activation(v_st, act_t[:, T_SV + kv, :], ACT.Copy).then_inc(sem("v_staged"), 1)
            act.wait_ge(sem("v_turned"), v)
            act.activation(v_tok, ps[:, 2, 0:T], ACT.Copy).then_inc(sem("v_tok_ready"), 1)
            more(0)
            act.wait_ge(sem("max_ready"), v)
            for i in range(REP):
                for b in range(2):
                    pr = prob[:, i, 0:P] if b == 0 else prob[:, i, P:3 * P]
                    act.activation(pr, pr, ACT.Exp, bias=soft[:, 1, i, b:b + 1],
                                   accum_out=soft[:, 3, i, b:b + 1])
            act.activation(soft[:, 2], soft[:, 2], ACT.Exp).then_inc(sem("exps_done"), 1)
            more(1, 2, 3)
            init(0)
            act.wait_ge(sem("p_turned"), v)
            for i in range(REP):
                ins = act.activation(prob_t[:, i, :], ps[:, 5 + i, 0:3 * P], ACT.Copy)
            ins.then_inc(sem("prob_t_ready"), 1)
            more(4, 5, 6, 7)
            init(1)

        def pool_act(act, l):
            act.wait_ge(sem("pool_mixed"), l + 1)
            for g in range(NPOOL):
                ins = act.activation(act_t[:, T_POOL + g, :], ps[:, g // 2, (g % 2) * T:(g % 2 + 1) * T],
                                     ACT.Copy, scale=par[:, R_PS + g:R_PS + g + 1])
            ins.then_inc(sem("pool_out"), 1)

        def delta_act(act, l, g, more, init):
            v = l * NG + g + 1
            act.wait_ge(sem("delta_out"), v)
            act.wait_ge(sem("evacuated"), l * A_PAIRS + 4 * g + (P_GROUP + 4 + 2))
            for dst, t0 in ((q_s, T_QKV), (k_s, T_QKV + DN_H), (v_s, T_QKV + 2 * DN_H), (z_s, T_Z)):
                act.activation(dst, act_t[:, bass.ds(2 * g + t0, 2), :].rearrange("p a n -> p (a n)"),
                               ACT.Silu).then_inc(sem("dn_silued"), 1)
            act.wait_ge(sem("qkv_turned"), 3 * v - 1)
            act.activation(e1, ps[:, 2, :], ACT.Square)
            act.activation(e2, ps[:, 3, :], ACT.Square).then_inc(sem("qk_squared"), 1)
            more(0, 1)
            for i, dst in enumerate((kn_t, qn_t, qd_t)):
                act.wait_ge(sem("normed_turned"), 3 * v - 2 + i)
                act.activation(dst, ps[:, 5 + i, :], ACT.Copy).then_inc(sem("normed_copied"), 1)
            more(2)
            act.wait_ge(sem("decay_arg"), v)
            act.activation(e1, e1, ACT.Exp, scale=-1.0)
            act.activation(e2, e2, ACT.Exp).then_inc(sem("decayed"), 1)
            more(3, 4)
            init(0)
            act.wait_ge(sem("n_turned"), v)
            act.activation(pw_t, ps[:, 5, :], ACT.Copy).then_inc(sem("nt_copied"), 1)
            more(5)
            for k in range(5):
                act.wait_ge(sem("squared"), 5 * v - 4 + k)
                act.activation(pw, ps[:, 3, :], ACT.Copy).then_inc(sem("pw_copied"), 1)
                more(6 + k)
                if k == 1:
                    init(1)
            more(11)
            act.wait_ge(sem("uw_done"), v)
            act.activation(u_m, ps[:, 5, :], ACT.Copy).then_inc(sem("u_copied"), 1)
            init(2)
            more(12, 13, 14)
            act.wait_ge(sem("o_done"), v)
            act.activation(o_m, ps[:, 6, :], ACT.Copy)
            act.activation(e2, ps[:, 6, :], ACT.Square).then_inc(sem("o_squared"), 1)
            more(15)
            init(3)

        def gates_dve(dve, l):
            dve.drain()
            dve.tensor_tensor(gtmp[:, 0], ba[:, :, DN_H:NBA].rearrange("p t h -> p h t"),
                              heads[:, 1, :].unsqueeze(2).broadcast_to([P, DN_H, TT]), ALU.add)
            dve.drain().then_inc(sem("gate_x"), 1)
            dve.wait_ge(sem("gate_abs"), l + 1)
            dve.tensor_scalar(gtmp[:, 0], gtmp[:, 0], 0.0, None, ALU.max)
            dve.wait_ge(sem("gate_ln"), l + 1)
            dve.tensor_scalar(gtmp[:, 2], gtmp[:, 2], 1.0, None, ALU.add)
            dve.drain()
            dve.tensor_tensor(gtmp[:, 0], gtmp[:, 0], gtmp[:, 1], ALU.add)
            dve.reciprocal(gate[:, 2], gtmp[:, 2])
            dve.drain()
            dve.scalar_tensor_tensor(gate[:, 0], gtmp[:, 0], -1.0,
                                     heads[:, 0, :].unsqueeze(2).broadcast_to([P, DN_H, TT]), ALU.mult, ALU.mult)
            dve.drain().then_inc(sem("gate_g_ready"), 1)

        def decays_dve(dve, l):
            dve.wait_ge(sem("gate_summed"), l + 1)
            dve.tensor_copy(gate[:, 1].rearrange("p h t -> p (h t)"), ps[:, 2, 0:12])
            dve.drain()
            dve.tensor_tensor(gtmp[:, 3].rearrange("p h t -> p (h t)"), ps[:, 2, 12:24],
                              gate[:, 1].rearrange("p h t -> p (h t)"), ALU.subtract)
            dve.drain().then_inc(sem("gate_sums"), 1)

        def rope_dve(dve, l, kv):
            q3 = act_t[:, T_SQ + 3 * kv:T_SQ + 3 * kv + 3, :]
            k1 = act_t[:, T_SK + kv:T_SK + kv + 1, :]
            dve.drain()
            for src, c0, n in ((q3, 0, 3), (k1, 3, 1)):
                for to, of in ((0, 64), (64, 0)):
                    dve.tensor_tensor(rope_x[to:to + 64, c0:c0 + n, :], src[of:of + 64],
                                      sin_t[of:of + 64, :].unsqueeze(1).broadcast_to([64, n, T]), ALU.mult)
                dve.tensor_tensor(roped[:, c0:c0 + n, :], src, cos_t[:].unsqueeze(1).broadcast_to([P, n, T]),
                                  ALU.mult)
            dve.drain()
            dve.tensor_tensor(roped, roped, rope_x, ALU.add).then_inc(sem("roped"), 1)

        def swa_dve(dve, l, kv, more, finish):
            v = l * SWA_KV + kv + 1
            dve.wait_ge(sem("scores_done"), v)
            dve.scalar_tensor_tensor(prob, ps[:, 3:6, 0:3 * P], QSCALE,
                                     const[:, C_SWA:C_SWA + 3 * P].unsqueeze(1).broadcast_to([P, REP, 3 * P]),
                                     ALU.mult, ALU.add)
            dve.drain()
            dve.tensor_reduce(soft[:, 0, :, 0], prob[:, :, 0:P], AX.X, ALU.max)
            dve.tensor_reduce(soft[:, 0, :, 1], prob[:, :, P:3 * P], AX.X, ALU.max)
            dve.drain()
            sinks = heads[:, 2, 3 * kv:3 * kv + 3].unsqueeze(2).broadcast_to([P, REP, 2])
            dve.tensor_tensor(soft[:, 0], soft[:, 0], sinks, ALU.max)
            dve.drain()
            dve.tensor_scalar(soft[:, 1], soft[:, 0], -1.0, None, ALU.mult)
            dve.tensor_tensor(soft[:, 2], sinks, soft[:, 0], ALU.subtract)
            dve.drain().then_inc(sem("max_ready"), 1)
            more(0)
            dve.wait_ge(sem("exps_done"), v)
            dve.tensor_tensor(soft[:, 3], soft[:, 3], soft[:, 2], ALU.add)
            dve.drain()
            dve.reciprocal(soft[:, 3], soft[:, 3])
            dve.drain()
            for b, sl in ((0, slice(0, P)), (1, slice(P, 3 * P))):
                n = P * (b + 1)
                dve.tensor_tensor(prob[:, :, sl], prob[:, :, sl],
                                  soft[:, 3, :, b].unsqueeze(2).broadcast_to([P, REP, n]), ALU.mult)
            dve.drain().then_inc(sem("p_ready"), 1)
            more(1, 2, 3)
            finish(0)
            if kv + 1 < SWA_KV:
                rope_dve(dve, l, kv + 1)
            more(4, 5)
            dve.wait_ge(sem("pv_done"), v)
            dve.tensor_copy(act_t[:, T_SQ + 3 * kv:T_SQ + 3 * kv + 2, :].rearrange("p a n -> p (a n)"), ps[:, 3, :])
            dve.tensor_copy(act_t[:, T_SQ + 3 * kv + 2, :], ps[:, 4, 0:T])
            dve.drain().then_inc(sem("swa_out"), 1)
            more(6, 7)
            finish(1)

        def delta_dve(dve, l, g, more, finish):
            v = l * NG + g + 1
            dve.drain()
            dve.tensor_copy(gate_g[:], gate[:, :, bass.ds(2 * g, 2), :].rearrange("p v h t -> p v (h t)"))
            dve.drain()
            G, GC, BETA, EG, KD = (gate_g[:, i, :] for i in range(5))
            dve.wait_ge(sem("dn_silued"), 4 * v)
            dve.tensor_copy(mats(gb), over(G)).then_inc(sem("g_spread"), 1)
            dve.wait_ge(sem("qk_squared"), v)
            dve.tensor_reduce(vec[:, 0, :], mats(e1), AX.X, ALU.add)
            dve.tensor_reduce(vec[:, 1, :], mats(e2), AX.X, ALU.add)
            dve.tensor_tensor(vec[:, 6, :], BETA, EG, ALU.mult)
            dve.tensor_scalar(vec[:, 10, :], BETA, -1.0, None, ALU.mult)
            dve.drain()
            dve.tensor_scalar(vec[:, 0:2, :], vec[:, 0:2, :], EPS, None, ALU.add)
            dve.drain().then_inc(sem("qk_ms"), 1)
            dve.wait_ge(sem("qk_rs"), v)
            dve.tensor_tensor(mats(kn), mats(ps[:, 3, :]), over(vec[:, 3, :]), ALU.mult).then_inc(sem("normed"), 1)
            dve.tensor_scalar(vec[:, 4, :], vec[:, 2, :], QSCALE, None, ALU.mult)
            dve.tensor_tensor(vec[:, 6, :], vec[:, 6, :], vec[:, 3, :], ALU.mult)
            dve.tensor_tensor(vec[:, 7, :], KD, vec[:, 3, :], ALU.mult)
            dve.drain()
            dve.tensor_tensor(mats(qn), mats(ps[:, 2, :]), over(vec[:, 4, :]), ALU.mult).then_inc(sem("normed"), 1)
            dve.tensor_tensor(vec[:, 5, :], vec[:, 4, :], EG, ALU.mult)
            dve.drain()
            dve.tensor_tensor(mats(qd), mats(ps[:, 2, :]), over(vec[:, 5, :]), ALU.mult).then_inc(sem("normed"), 1)
            more(0)
            dve.tensor_tensor(mats(kbeg), mats(ps[:, 3, :]), over(vec[:, 6, :]), ALU.mult)
            dve.tensor_tensor(mats(kdec), mats(ps[:, 3, :]), over(vec[:, 7, :]), ALU.mult)
            dve.wait_ge(sem("qkv_turned"), 3 * v)
            dve.tensor_tensor(mats(vb), mats(ps[:, 4, :]), over(BETA), ALU.mult)
            dve.drain().then_inc(sem("scaled"), 1)
            more(1)
            dve.wait_ge(sem("gc_rows"), v)
            dve.tensor_tensor(mats(gb), mats(ps[:, 2, :]), over(GC), ALU.subtract)
            dve.drain()
            dve.tensor_scalar(e1, gb, 0.0, None, ALU.max)
            dve.tensor_scalar(e2, gb, 0.0, None, ALU.min)
            dve.drain().then_inc(sem("decay_arg"), 1)
            more(2)
            dve.wait_ge(sem("decayed"), v)
            for m in range(4):
                em = mats(e1)[:, m, :]
                dve.scalar_tensor_tensor(em, em, vec[:, 10, m:m + 1], lower, ALU.mult, ALU.mult)
            dve.tensor_tensor(mats(e2), mats(e2), upper.unsqueeze(1).broadcast_to([P, 4, P]), ALU.mult)
            dve.drain()
            dve.wait_ge(sem("kk_done"), v)
            dve.tensor_tensor(pw, ps[:, 3, :], e1, ALU.mult).then_inc(sem("n_ready"), 1)
            dve.wait_ge(sem("qk_done"), v)
            dve.tensor_tensor(attn, ps[:, 4, :], e2, ALU.mult).then_inc(sem("attn_ready"), 1)
            more(3)
            finish(0)
            dve.wait_ge(sem("nt_copied"), v)
            dve.tensor_tensor(mats(inv), mats(pw_t), ident.unsqueeze(1).broadcast_to([P, 4, P]),
                              ALU.add).then_inc(sem("inv_ready"), 1)
            for k in range(5):
                if k < 4:
                    if k == 0:
                        dve.drain()
                    dve.wait_ge(sem("squared"), 5 * v - 4 + k)
                    dve.tensor_copy(pw_t, ps[:, 4, :]).then_inc(sem("pwt_copied"), 1)
                more(4 + k)
                dve.wait_ge(sem("inv_product"), 5 * v - 4 + k)
                dve.tensor_tensor(inv, inv, ps[:, 6, :], ALU.add).then_inc(sem("inv_ready"), 1)
                if k == 3:
                    finish(1)
            more(9)
            dve.wait_ge(sem("uw_done"), v)
            dve.tensor_copy(w_t, ps[:, 7, :])
            dve.memset(state, 0.0)
            dve.drain().then_inc(sem("state_ready"), 1)
            more(10, 11)
            dve.wait_ge(sem("u_copied"), v)
            for n in range(4):
                t, c = n // 2, n % 2
                r = slice(CH * c, CH * (c + 1))
                dve.wait_ge(sem("ws_done"), 4 * v - 3 + n)
                dve.tensor_tensor(v_new[r, :].rearrange("p (h n) -> p h n", h=2), mats(u_m)[r, t::2, :],
                                  ps[r, 2, 0:256].rearrange("p (h n) -> p h n", h=2),
                                  ALU.subtract).then_inc(sem("v_new_ready"), 1)
                if n < 3:
                    dve.wait_ge(sem("state_add"), 3 * v - 2 + n)
                    for h in range(2):
                        sh = state[:, h * P:(h + 1) * P]
                        dve.scalar_tensor_tensor(sh, sh, gate_g[:, 5 + c, 2 * h + t:2 * h + t + 1],
                                                 ps[:, 3, h * P:(h + 1) * P], ALU.mult, ALU.add)
                    dve.drain().then_inc(sem("state_ready"), 1)
                    if n == 0:
                        finish(2)
                    more(12 + n)
            dve.wait_ge(sem("o_squared"), v)
            dve.tensor_reduce(vec[:, 8, :], mats(e2), AX.X, ALU.add)
            dve.drain()
            dve.tensor_scalar(vec[:, 8, :], vec[:, 8, :], 1.0 / HD, EPS, ALU.mult, ALU.add)
            dve.drain().then_inc(sem("o_ms"), 1)
            dve.wait_ge(sem("o_rs"), v)
            dve.tensor_tensor(mats(o_m), mats(o_m), over(vec[:, 9, :]), ALU.mult).then_inc(sem("o_ready"), 1)
            dve.wait_ge(sem("o_turned"), v)
            dve.scalar_tensor_tensor(act_t[:, bass.ds(2 * g, 2), :].rearrange("p a n -> p (a n)"), ps[:, 4, :],
                                     par[:, R_DNW:R_DNW + 1], z_s, ALU.mult, ALU.mult)
            dve.drain().then_inc(sem("delta_out"), 1)
            more(15)
            finish(3)

        def gates_pe(pe, l):
            pe.wait_ge(sem("gate_g_ready"), l + 1)
            gm = gate[:, 0].rearrange("p h t -> p (h t)")
            chunk0, chunk1 = (block[:, CH * c:CH * c + 1].broadcast_to([P, P]) for c in range(2))
            for i, w in enumerate((upper, block, chunk0, chunk1)):
                ins = pe.matmul(ps[:, 2, 12 * i:12 * (i + 1)], w, gm, start=True, stop=True)
            ins.then_inc(sem("gate_summed"), 1)

        def swa_pe(pe, l, kv, more):
            v = l * SWA_KV + kv + 1
            pe.wait_ge(sem("swa_out"), v)
            pe.wait_ge(sem("v_staged"), v)
            for t in range(TT):
                ins = pe.transpose(ps[:, 2, t * P:(t + 1) * P], v_st[:, t * P:(t + 1) * P], ident)
            ins.then_inc(sem("v_turned"), 1)
            pe.wait_ge(sem("roped"), v)
            for i in range(REP):
                pe.matmul(ps[:, 3 + i, 0:P], roped[:, i, 0:P], roped[:, 3, 0:P], start=True, stop=True)
                ins = pe.matmul(ps[:, 3 + i, P:3 * P], roped[:, i, P:T], roped[:, 3, :], start=True, stop=True)
            ins.then_inc(sem("scores_done"), 1)
            more(0, 1, 2, 3)
            pe.wait_ge(sem("p_ready"), v)
            for i in range(REP):
                for b in range(3):
                    ins = pe.transpose(ps[:, 5 + i, b * P:(b + 1) * P], prob[:, i, b * P:(b + 1) * P], ident)
            ins.then_inc(sem("p_turned"), 1)
            more(4, 5)
            pe.wait_ge(sem("v_tok_ready"), v)
            pe.wait_ge(sem("prob_t_ready"), v)
            for i in range(REP):
                bank, c = 3 + i // 2, (i % 2) * T
                pt = prob_t[:, i, :]
                pe.matmul(ps[:, bank, c:c + P], v_tok[:, 0:P], pt[:, 0:P], start=i != 1, stop=True,
                          skip_group_check=True)
                pe.matmul(ps[:, bank, c + P:c + T], v_tok[:, 0:P], pt[:, P:2 * P], start=False, stop=False,
                          skip_group_check=True)
                ins = pe.matmul(ps[:, bank, c + P:c + T], v_tok[:, P:T], pt[:, 2 * P:3 * P], start=False,
                                stop=True, skip_group_check=True)
            ins.then_inc(sem("pv_done"), 1)
            more(6, 7)

        def pool_pe(pe, l):
            pe.wait_ge(sem("pooled"), l + 1)
            for g in range(NPOOL):
                ins = pe.matmul(ps[:, g // 2, (g % 2) * T:(g % 2 + 1) * T], pool_w[:, g, :],
                                win[(g + 1) % 2][:, g, 16:], start=True, stop=True)
            ins.then_inc(sem("pool_mixed"), 1)

        def delta_pe(pe, l, g, more):

            def four(bank, w, r):
                w, r = mats(w), mats(r)
                for m in range(4):
                    ins = pe.matmul(ps[:, bank, m * P:(m + 1) * P], w[:, m, :], r[:, m, :], start=True, stop=True)
                return ins

            def turn(bank, src):
                for m in range(4):
                    ins = pe.transpose(ps[:, bank, m * P:(m + 1) * P], mats(src)[:, m, :], ident)
                return ins

            v = l * NG + g + 1
            pe.wait_ge(sem("delta_out"), v)
            for i, src in enumerate((q_s, k_s, v_s)):
                pe.wait_ge(sem("dn_silued"), 4 * v - 3 + i)
                turn(2 + i, src).then_inc(sem("qkv_turned"), 1)
            more(0, 1)
            for i, src in enumerate((kn, qn, qd)):
                pe.wait_ge(sem("normed"), 3 * v - 2 + i)
                turn(5 + i, src).then_inc(sem("normed_turned"), 1)
            more(2)
            pe.wait_ge(sem("g_spread"), v)
            pe.wait_ge(sem("scaled"), v)
            for m in range(4):
                ins = pe.matmul(ps[:, 2, m * P:(m + 1) * P], mats(gb)[:, m, :], upper, start=True, stop=True)
            ins.then_inc(sem("gc_rows"), 1)
            pe.wait_ge(sem("normed_copied"), 3 * v - 1)
            four(3, kn_t, kn_t).then_inc(sem("kk_done"), 1)
            four(4, kn_t, qn_t).then_inc(sem("qk_done"), 1)
            more(3, 4)
            pe.wait_ge(sem("n_ready"), v)
            turn(5, pw).then_inc(sem("n_turned"), 1)
            more(5)
            pe.wait_ge(sem("attn_ready"), v)
            for k in range(5):
                if k == 0:
                    pe.wait_ge(sem("nt_copied"), v)
                else:
                    pe.wait_ge(sem("pwt_copied"), 4 * v - 4 + k)
                ins = four(3, pw_t, pw)
                if k < 4:
                    ins = four(4, pw, pw_t)
                ins.then_inc(sem("squared"), 1)
                more(6 + k)
                pe.wait_ge(sem("pw_copied"), 5 * v - 4 + k)
                pe.wait_ge(sem("inv_ready"), 6 * v - 5 + k)
                four(6, pw, inv).then_inc(sem("inv_product"), 1)
            more(11)
            pe.wait_ge(sem("inv_ready"), 6 * v)
            pe.wait_ge(sem("normed_copied"), 3 * v)
            four(5, inv, vb)
            four(7, kbeg, inv).then_inc(sem("uw_done"), 1)
            more(12)
            for n in range(4):
                t, c = n // 2, n % 2
                r = slice(CH * c, CH * (c + 1))
                pe.wait_ge(sem("state_ready"), 4 * v - 3 + n)
                for h in range(2):
                    m = 2 * h + t
                    cols = slice(m * P + CH * c, m * P + CH * (c + 1))
                    ins = pe.matmul(ps[r, 2, h * P:(h + 1) * P], w_t[:, cols], state[:, h * P:(h + 1) * P],
                                    start=True, stop=True)
                ins.then_inc(sem("ws_done"), 1)
                for h in range(2):
                    m = 2 * h + t
                    cols = slice(m * P + CH * c, m * P + CH * (c + 1))
                    pe.matmul(ps[r, 6, m * P:(m + 1) * P], qd_t[:, cols], state[:, h * P:(h + 1) * P],
                              start=h == 0, stop=False, skip_group_check=True)
                if n in (0, 2):
                    more(13 + n // 2)
                hold(pe, sem("v_new_ready"), 4 * v - 3 + n)
                if n < 3:
                    for h in range(2):
                        m = 2 * h + t
                        ins = pe.matmul(ps[:, 3, h * P:(h + 1) * P], kdec[r, m * P:(m + 1) * P],
                                        v_new[r, h * P:(h + 1) * P], start=True, stop=True)
                    ins.then_inc(sem("state_add"), 1)
                for h in range(2):
                    m = 2 * h + t
                    cols = slice(m * P + CH * c, m * P + CH * (c + 1))
                    ins = pe.matmul(ps[r, 6, m * P:(m + 1) * P], attn[r, cols], v_new[r, h * P:(h + 1) * P],
                                    start=False, stop=True, skip_group_check=True)
                if n == 3:
                    ins.then_inc(sem("o_done"), 1)
            more(15)
            pe.wait_ge(sem("o_ready"), v)
            turn(4, o_m).then_inc(sem("o_turned"), 1)

        @blk.sync
        def _(sp):
            sp.dma_start(const[:], a["consts"]).then_inc(sem("const_in"), 16)
            sp.dma_start(scr[:, 0, 0:T].bitcast(I32),
                         a["positions"].broadcast_to([P, T])).then_inc(sem("pos_in"), 16)
            sp.dma_start(x[:], a["x"].rearrange("b (t p) d -> p (b t) d", p=P)).then_inc(sem("x_in"), 16)

            def pair(l, q, j, dst, src):
                sp.wait_ge(lo_done, l * SUBS + 8 * j + (4 * q + 4))
                sp.dma_start(dst, src).then_inc(landed[q % 2], 16)

            def form_a(l, q, j, w, col):
                pair(l, q, j, raw_a[:, q % 2, :, :],
                     w[at(l), :, :, bass.ds(col, 256)].rearrange("l p k n -> (l p) k n"))

            def form_b(l, q, j, w, k):
                pair(l, q, j, raw_b[:, q % 2, :, :],
                     w[at(l), :, bass.ds(k, 2), :].rearrange("l p k n -> (l p) k n"))

            def post_weights(l, name):
                sp.dma_start(w_post.rearrange("p a n -> p (a n)"),
                             a[name][at(l), :].broadcast_to([P, D])).then_inc(sem("post_w_in"), 16)

            with sp.Fori(0, DEPTH) as l:
                sp.wait_ge(sem("mixed"), l + 1)
                dnc = a["dn_conv_w"].rearrange("l k (r c) -> l (k r) c", c=P)
                loads = [(rows1[r:r + n, :], v[at(l), :, :].rearrange("l r c -> (l r) c")) for r, n, v in (
                    (R_PRE, KT, a["norm_mix_pre"].rearrange("l (r c) -> l r c", c=P)),
                    (R_FFN, KT, a["norm_ffn_pre"].rearrange("l (r c) -> l r c", c=P)),
                    (R_DNC, DN_TAPS * DN_TILES, dnc),
                    (R_PS, NPOOL, a["pool_scale"].rearrange("l (r c) -> l r c", c=P)),
                    (R_DNW, 1, a["dn_norm_w"].rearrange("l (r c) -> l r c", c=P)))]
                fc = a["ffn_conv_w"].rearrange("l k (r c) -> l (k r) c", c=P)
                fb = a["ffn_conv_b"].rearrange("l (r c) -> l r c", c=P)
                loads += [(rows2[p0:p0 + r1 - r0, b, :], src[at(l), r0:r1, :].rearrange("l r c -> (l r) c"))
                          for src, r0, r1, b, p0 in ((fc, 0, 128, 0, 0), (fc, 128, 256, 1, 0),
                                                     (fc, 256, 264, 2, 0), (fb, 0, 88, 2, 8))]
                loads += [(heads[:, i, :], a[name][at(l), :].broadcast_to([P, DN_H]))
                          for i, name in enumerate(("dn_a_log", "dn_dt_bias", "swa_sinks"))]
                loads.append((pool_w[:], a["pool_w"][at(l)].rearrange("l g c d -> (l c) g d")))
                assert len(loads) == N_PARAM_DMAS
                for dst, src in loads:
                    sp.dma_start(dst, src).then_inc(sem("params_in"), 16)

                pair(l, 0, 0, raw[:, 0, 0:KT * NBA].rearrange("p (k n) -> p k n", n=NBA),
                     w_in[at(l), :, :, COL_BA:COL_BA + NBA].rearrange("l p k n -> (l p) k n"))
                for i, (col, _) in enumerate(HEAD):
                    form_a(l, 1 + i, 0, w_in, col)
                with sp.Fori(0, NG) as g:
                    for i in range(4):
                        form_a(l, P_GROUP + i, 2 * g, w_in, 256 * g + DN_H * HD * i)
                form_a(l, P_POOL, 0, w_in, COL_POOL)
                form_a(l, P_POOL + 1, 0, w_in, COL_POOL + 256)
                with sp.Fori(0, N_OUT // 2) as j:
                    form_b(l, P_OUT, j, w_out, 4 * j)
                    form_b(l, P_OUT + 1, j, w_out, 4 * j + 2)
                sp.wait_ge(sem("mixed"), l + 2)
                post_weights(l, "norm_mix_post")
                with sp.Fori(0, N_UP // 2) as j:
                    form_a(l, P_UP, j, w_up, 256 * j)
                    form_a(l, P_UP + 1, j, w_up, 256 * j + FF)
                sp.wait_ge(sem("x_new"), 4 * l + 6)
                post_weights(l, "norm_ffn_post")
                with sp.Fori(0, N_DOWN // 2) as j:
                    form_b(l, P_DOWN, j, w_down, 4 * j)
                    form_b(l, P_DOWN + 1, j, w_down, 4 * j + 2)
            sp.wait_ge(sem("x_new"), 4 * DEPTH + 4)
            sp.dma_start(out.rearrange("b (t p) d -> p (b t) d", p=P), x[:]).then_inc(sem("stored"), 16)
            sp.wait_ge(sem("stored"), 16)

        @blk.gpsimd
        def _(pool):
            pool.memset(mhalf[:], -0.5).then_inc(sem("mhalf_set"), 1)
            pool.wait_ge(sem("mhalf_set"), 1)

            def root(dst, src, n, of, value, done):
                pool.wait_ge(sem(of), value)
                pool.tensor_tensor(dst, src, mhalf[:, 0:n], ALU.pow).then_inc(sem(done), 1)

            def norm_roots(kind, l, f, s, d):
                for t in range(TT):
                    root(small[:, d + t:d + t + 1], small[:, s + t:s + t + 1], 1,
                         kind + "_ms", 4 * l + (2 * f + t + 1), kind + "_rs")

            def windows(l):
                hold(pool, sem("evacuated"), l * A_PAIRS + (N_IN + 2))
                hold(pool, sem("dn_silued"), 4 * NG * l + 4 * NG)
                pool.memset(win[0][:, :, 0:16], 0.0)
                pool.memset(win[1][:, :, 0:16], 0.0)
                pool.tensor_copy(win[0][:, :, 16:], act_t[:, T_POOL:T_POOL + NPOOL, :])
                for i in range(NPOOL):
                    src, dst = win[i % 2], win[(i + 1) % 2]
                    pool.drain()
                    pool.tensor_tensor(dst[:, i:, 16:], src[:, i:, 16:], src[:, i:, 16 - 2 ** i:16 + T - 2 ** i],
                                       ALU.add)
                pool.drain()
                for g in range(NPOOL):
                    w = win[(g + 1) % 2][:, g, 16:32]
                    pool.tensor_tensor(w, w, const[:, C_COR + 16 * g:C_COR + 16 * (g + 1)], ALU.mult)
                pool.drain()
                for g in range(NPOOL):
                    w = win[(g + 1) % 2][:, g, 16:]
                    pool.tensor_scalar(w, w, 1.0 / WINDOWS[g], None, ALU.mult)
                pool.drain()
                for g in range(NPOOL):
                    w = win[(g + 1) % 2][:, g, 16:]
                    pool.tensor_tensor(w, w, act_t[:, T_POOL + g, :], ALU.subtract)
                pool.drain().then_inc(sem("pooled"), 1)

            with pool.Fori(0, DEPTH) as l:
                norm_roots("pre", l, 0, 24, 28)
                with pool.Fori(0, NG - 1) as g:
                    root(vec[:, 2:4, :].rearrange("p a n -> p (a n)"), vec[:, 0:2, :].rearrange("p a n -> p (a n)"),
                         8, "qk_ms", l * NG + g + 1, "qk_rs")
                    root(vec[:, 9, :], vec[:, 8, :], 4, "o_ms", l * NG + g + 1, "o_rs")
                root(vec[:, 2:4, :].rearrange("p a n -> p (a n)"), vec[:, 0:2, :].rearrange("p a n -> p (a n)"),
                     8, "qk_ms", l * NG + NG, "qk_rs")
                windows(l)
                root(vec[:, 9, :], vec[:, 8, :], 4, "o_ms", l * NG + NG, "o_rs")
                norm_roots("post", l, 0, 16, 20)
                norm_roots("pre", l, 1, 24, 28)
                norm_roots("post", l, 1, 16, 20)

        @blk.scalar
        def _(act):
            def hi(l, q, j=0, n=1024):
                for s in range(4):
                    hi_part(l, q, j, s, n)

            def hi_part(l, q, j, s, n=1024):
                if s == 0:
                    act.wait_ge(landed[q % 2], l * (PAIRS // 2 * 16) + 16 * j + 16 * (q // 2 + 1))
                act.wait_ge(sub_used, l * SUBS + 8 * j + (4 * q + s + 1))
                act.activation(w_hi[:, s, 0:n], raw[:, q % 2, s * n:(s + 1) * n], ACT.Copy).then_inc(hi_done, 1)

            def pre_norm(l, f, col):
                for t in range(TT):
                    act.wait_ge(sem("x_new"), 4 * l + (3 + 2 * f + t))
                    act.activation(h_tok[:, t, :], x[:, t, :], ACT.Square,
                                   accum_out=small[:, 22 + t:23 + t]).then_inc(sem("pre_ssq"), 1)
                for b in range(8):
                    act.wait_ge(sem("h_turned"), 16 * l + (8 * f + b + 1))
                    for i in range(2):
                        k = 2 * b + i
                        ins = act.activation(h_hi[:, k, :], ps[:, b, i * T:(i + 1) * T], ACT.Copy,
                                             scale=par[:, col + k:col + k + 1])
                    ins.then_inc(sem("h_hi_done"), 1)

            def post_norm(l, q_last):
                act.wait_ge(sub_used, sub_count(l, q_last))
                for t in range(TT):
                    for c in range(4):
                        ins = act.activation(h_tok[:, t, c * 512:(c + 1) * 512], ps[:, 4 * t + c, :], ACT.Square,
                                             accum_out=small[:, 4 * t + c:4 * t + c + 1])
                    ins.then_inc(sem("post_ssq"), 1)

            def x_hi(l, q, j, k, first=False):
                act.wait_ge(sub_used, l * SUBS + 8 * j + 4 * (first if first else q))
                act.activation(h_hi[:, 2 * (q % 2):2 * (q % 2) + 2, :], act_t[:, bass.ds(k, 2), :],
                               ACT.Copy).then_inc(sem("x_hi_done"), 1)

            def form_b(l, base, n):
                x_hi(l, base, 0, 0, base + 1)
                x_hi(l, base + 1, 0, 2, base + 1)
                hi(l, base + 1)
                with act.Fori(0, n // 2 - 1) as j:
                    for i in range(2):
                        x_hi(l, base + 2 + i, j, 4 * j + (4 + 2 * i))
                        hi(l, base + 2 + i, j)

            act.wait_ge(sem("angle_ready"), 1)
            act.activation(sin_t[:], scr[:, 1, 0:T], ACT.Sin).then_inc(sem("sined"), 1)
            act.activation(cos_t[:], scr[:, 1, 0:T], ACT.Sin, scale=0.5).then_inc(sem("sined"), 1)

            with act.Fori(0, DEPTH) as l:
                hi(l, 0, 0, KT * NBA // 4)
                pre_norm(l, 0, R_PRE)
                for q in range(1, P_GROUP + 1):
                    hi(l, q)
                    if q == 2:
                        gates_act(act, l)
                    if q == 4:
                        decays_act(act, l)

                def more_of(q, j, n_parts):
                    def more(*parts):
                        for n in parts:
                            if n < n_parts:
                                hi_part(l, q + (n + 4) // 4, j, n % 4)
                    return more

                def conv_init(q, j, tile):
                    act.wait_ge(sub_used, sub_count(l, q, j))
                    for i in range(2):
                        ins = act.activation(act_t[:, bass.ds(tile + (T_QKV + i), 1), :].rearrange("p a n -> p (a n)"),
                                             ps[:, q % 2, i * T:(i + 1) * T], ACT.Copy,
                                             scale=par[:, bass.ds(tile + (R_DNC + 3 * DN_TILES + i), 1)])
                    ins.then_inc(sem("conv_init"), 1)

                for kv in range(SWA_KV):
                    q = P_GROUP + 2 * kv

                    def init(i):
                        if 2 * kv + i < 3:
                            conv_init(q + i, 0, DN_H * (2 * kv + i))
                    swa_act(act, l, kv, more_of(q, 0, 8), init)
                act.wait_ge(sem("swa_out"), l * SWA_KV + SWA_KV + 1)
                with act.Fori(0, NG - 1) as g:
                    def init(i):
                        if i < 3:
                            conv_init(P_GROUP + 4 + i, 2 * g, 2 * g + (DN_H * i + 2))
                    delta_act(act, l, g, more_of(P_GROUP + 4, 2 * g, 16), init)
                delta_act(act, l, NG - 1, more_of(P_POOL, 0, 8), lambda i: None)
                pool_act(act, l)
                act.wait_ge(sem("mixed"), l + 2)
                form_b(l, P_OUT, N_OUT)
                post_norm(l, P_OUT + N_OUT - 1)
                hi(l, P_UP)
                pre_norm(l, 1, R_FFN)
                hi(l, P_UP + 1)

                def ffn_init(l, j, ab):
                    act.wait_ge(sub_used, sub_count(l, P_UP + ab, j))
                    if ab == 0:
                        act.wait_ge(sem("hidden"), l * (FT // 2) + j + 1)
                    for i in range(2):
                        ins = act.activation(y_ab[:, ab, i, :], ps[:, ab, i * T:(i + 1) * T], ACT.Identity,
                                             scale=par[:, bass.ds(2 * j + (R_FC + 2 * 2 * FT + ab * FT + i), 1)],
                                             bias=par[:, bass.ds(2 * j + (R_FB + ab * FT + i), 1)])
                    ins.then_inc(sem("ffn_init"), 1)

                def silu(l, j):
                    act.wait_ge(sem("evacuated"), l * A_PAIRS + 2 * j + (N_IN + 1 + 2))
                    act.activation(y_ab[:, 0, :, :], y_ab[:, 0, :, :], ACT.Silu).then_inc(sem("silued"), 1)

                def up_step(l, j, last):
                    ffn_init(l, j, 0)
                    if not last:
                        hi(l, P_UP + 2, j)
                    silu(l, j)
                    ffn_init(l, j, 1)
                    if not last:
                        hi(l, P_UP + 3, j)

                act.preload_act_table_set("silu_and_others")
                with act.Fori(0, N_UP // 2 - 1) as j:
                    up_step(l, j, False)
                up_step(l, N_UP // 2 - 1, True)
                hi(l, P_DOWN)
                act.wait_ge(sem("hidden"), l * (FT // 2) + (FT // 2 + 1))
                form_b(l, P_DOWN, N_DOWN)
                post_norm(l, P_DOWN + N_DOWN - 1)

        @blk.vector
        def _(dve):
            def lo(l, q, j=0, n=1024):
                for s in range(4):
                    lo_part(l, q, j, s, n)

            def lo_part(l, q, j, s, n=1024):
                dve.wait_ge(hi_done, l * SUBS + 8 * j + (4 * q + s + 1))
                dve.tensor_tensor(w_lo[:, s, 0:n], raw[:, q % 2, s * n:(s + 1) * n],
                                  w_hi[:, s, 0:n].bitcast(F32), ALU.subtract).then_inc(lo_done, 1)

            def mean(kind, l, f, n, ssq, ms):
                for t in range(TT):
                    dve.wait_ge(sem(kind + "_ssq"), 4 * l + (2 * f + t + 1))
                    if n > 1:
                        dve.tensor_reduce(small[:, 32 + t:33 + t], small[:, ssq + n * t:ssq + n * t + n], AX.X, ALU.add)
                        dve.drain()
                        src = small[:, 32 + t:33 + t]
                    else:
                        src = small[:, ssq + t:ssq + t + 1]
                    dve.tensor_scalar(small[:, ms + t:ms + t + 1], src, 1.0 / D, EPS, ALU.mult,
                                      ALU.add).then_inc(sem(kind + "_ms"), 1)
                    yield t

            def pre_norm(l, f, col):
                for t in mean("pre", l, f, 1, 22, 24):
                    dve.wait_ge(sem("pre_rs"), 4 * l + (2 * f + t + 1))
                    dve.tensor_scalar(h_tok[:, t, :], x[:, t, :], small[:, 28 + t:29 + t], None,
                                      ALU.mult).then_inc(sem("h_ready"), 1)
                for b in range(8):
                    dve.wait_ge(sem("h_hi_done"), 16 * l + (8 * f + b + 1))
                    for i in range(2):
                        k = 2 * b + i
                        ins = dve.scalar_tensor_tensor(h_lo[:, k, :], ps[:, b, i * T:(i + 1) * T],
                                                       par[:, col + k:col + k + 1], h_hi[:, k, :].bitcast(F32),
                                                       ALU.mult, ALU.subtract)
                    ins.then_inc(sem("h_lo_done"), 1)

            def post_norm(l, f):
                for t in mean("post", l, f, 4, 0, 16):
                    dve.wait_ge(sem("post_rs"), 4 * l + (2 * f + t + 1))
                    if t == 0:
                        dve.wait_ge(sem("post_w_in"), 32 * l + 16 * (f + 1))
                    for c in range(4):
                        dve.scalar_tensor_tensor(h_tok[:, t, c * 512:(c + 1) * 512], ps[:, 4 * t + c, :],
                                                 small[:, 20 + t:21 + t], w_post[:, c, :], ALU.mult, ALU.mult)
                    dve.drain()
                    dve.tensor_tensor(x[:, t, :], x[:, t, :], h_tok[:, t, :], ALU.add).then_inc(sem("x_new"), 1)

            def x_lo(l, q, j, k, f, m):
                dve.wait_ge(sem("x_hi_done"), l * (N_OUT + N_DOWN) + f * N_OUT + 2 * j + (m + 1))
                sl = slice(2 * (q % 2), 2 * (q % 2) + 2)
                dve.tensor_tensor(h_lo[:, sl, :], act_t[:, bass.ds(k, 2), :], h_hi[:, sl, :].bitcast(F32),
                                  ALU.subtract).then_inc(sem("x_lo_done"), 1)

            def form_b(l, base, n, f):
                x_lo(l, base, 0, 0, f, 0)
                x_lo(l, base + 1, 0, 2, f, 1)
                lo(l, base + 1)
                with dve.Fori(0, n // 2 - 1) as j:
                    for i in range(2):
                        x_lo(l, base + 2 + i, j, 4 * j + (4 + 2 * i), f, 2 + i)
                        lo(l, base + 2 + i, j)

            dve.memset(small[:], 0.0)
            dve.drain().then_inc(lo_done, 8)
            for name, n in (("evacuated", 2), ("mixed", 1), ("hidden", 1), ("swa_out", 1), ("delta_out", 1)):
                dve.drain().then_inc(sem(name), n)

            dve.wait_ge(sem("const_in"), 16)
            dve.wait_ge(sem("pos_in"), 16)
            pos, ang, turns = scr[:, 2, 0:T], scr[:, 1, 0:T], scr[:, 3, 0:T]
            dve.tensor_copy(pos, scr[:, 0, 0:T].bitcast(I32))
            dve.drain()
            dve.tensor_scalar(ang, pos, const[:, C_INVF:C_INVF + 1], None, ALU.mult)
            dve.drain()
            dve.tensor_scalar(turns, ang, 1.0 / (2 * np.pi), MAGIC, ALU.mult, ALU.add)
            dve.drain()
            dve.tensor_scalar(turns, turns, MAGIC, None, ALU.subtract)
            dve.drain()
            for part in TWO_PI:
                dve.scalar_tensor_tensor(ang, turns, -part, ang, ALU.mult, ALU.add)
                dve.drain()
            dve.tensor_scalar(ang, ang, PI_IN, -PI_IN, ALU.min, ALU.max).then_inc(sem("angle_ready"), 1)
            dve.wait_ge(sem("sined"), 2)
            dve.tensor_scalar(sin_t[:], sin_t[:], const[:, C_SGN:C_SGN + 1], None, ALU.mult)
            dve.tensor_tensor(cos_t[:], cos_t[:], cos_t[:], ALU.mult)
            dve.drain()
            dve.tensor_scalar(cos_t[:], cos_t[:], -2.0, 1.0, ALU.mult, ALU.add)
            dve.wait_ge(sem("x_in"), 16)
            dve.drain().then_inc(sem("x_new"), 4)

            with dve.Fori(0, DEPTH) as l:
                dve.wait_ge(sem("params_turned"), l + 1)
                dve.tensor_copy(par[:, 0:R_ONE], ps[:, 0, 0:R_ONE])
                dve.tensor_copy(par[:, R_ONE:R_ALL], ps[:, 1, 0:FROWS])
                dve.drain().then_inc(sem("par_ready"), 1)
                lo(l, 0, 0, KT * NBA // 4)
                pre_norm(l, 0, R_PRE)
                lo(l, 1)
                dve.wait_ge(sub_used, sub_count(l, 0))
                dve.tensor_copy(ba[:].rearrange("p t n -> p (t n)"), ps[:, 0, 0:2 * NBA]).then_inc(sem("evacuated"), 1)
                gates_dve(dve, l)

                def copy_out(q, tile):
                    dve.wait_ge(sub_used, sub_count(l, q))
                    dve.tensor_copy(act_t[:, tile:tile + 2, :].rearrange("p a n -> p (a n)"),
                                    ps[:, q % 2, :]).then_inc(sem("evacuated"), 1)

                for i, (_, tile) in enumerate(HEAD):
                    lo(l, 2 + i)
                    copy_out(1 + i, tile)
                    if i == 1:
                        decays_dve(dve, l)

                def more_of(q, j, n_parts):
                    def more(*parts):
                        for n in parts:
                            if n < n_parts:
                                lo_part(l, q + (n + 4) // 4, j, n % 4)
                    return more

                def conv_taps(q, j, inits, tile):
                    dve.wait_ge(sem("conv_init"), l * 9 + inits)
                    for k in range(1, DN_TAPS):
                        if k > 1:
                            dve.drain()
                        for i in range(2):
                            y = act_t[:, bass.ds(tile + (T_QKV + i), 1), k:T].rearrange("p a n -> p (a n)")
                            ins = dve.scalar_tensor_tensor(
                                y, ps[:, q % 2, i * T:(i + 1) * T - k],
                                par[:, bass.ds(tile + (R_DNC + (3 - k) * DN_TILES + i), 1)], y, ALU.mult, ALU.add)
                    ins.then_inc(sem("evacuated"), 1)

                rope_dve(dve, l, 0)
                for kv in range(SWA_KV):
                    q = P_GROUP + 2 * kv

                    def finish(i):
                        if 2 * kv + i < 3:
                            conv_taps(q + i, 0, 2 * kv + i + 1, DN_H * (2 * kv + i))
                        else:
                            copy_out(q + i, T_Z)
                    swa_dve(dve, l, kv, more_of(q, 0, 8), finish)
                hold(dve, sem("gate_exp"), l + 1)
                with dve.Fori(0, NG - 1) as g:
                    def finish(i):
                        q = P_GROUP + 4 + i
                        if i < 3:
                            conv_taps(q, 2 * g, 3 * g + (4 + i), 2 * g + (DN_H * i + 2))
                        else:
                            dve.wait_ge(sub_used, sub_count(l, q, 2 * g))
                            dve.tensor_scalar(
                                act_t[:, bass.ds(2 * g + (T_Z + 2), 2), :].rearrange("p a n -> p (a n)"),
                                ps[:, q % 2, :], 1.0, None, ALU.mult).then_inc(sem("evacuated"), 1)
                    delta_dve(dve, l, g, more_of(P_GROUP + 4, 2 * g, 16), finish)

                def finish(i):
                    if i < 2:
                        copy_out(P_POOL + i, T_POOL + 2 * i)
                delta_dve(dve, l, NG - 1, more_of(P_POOL, 0, 8), finish)
                hold(dve, sem("pool_out"), l + 1)
                dve.drain().then_inc(sem("mixed"), 1)

                form_b(l, P_OUT, N_OUT, 0)
                post_norm(l, 0)
                lo(l, P_UP)
                pre_norm(l, 1, R_FFN)
                lo(l, P_UP + 1)

                def taps(l, j, ab):
                    dve.wait_ge(sem("ffn_init"), l * N_UP + 2 * j + (ab + 1))
                    for k in range(1, FFN_TAPS):
                        if k > 1:
                            dve.drain()
                        for i in range(2):
                            y = y_ab[:, ab, i, k:T]
                            ins = dve.scalar_tensor_tensor(
                                y, ps[:, ab, i * T:(i + 1) * T - k],
                                par[:, bass.ds(2 * j + (R_FC + (2 - k) * 2 * FT + ab * FT + i), 1)], y,
                                ALU.mult, ALU.add)
                    ins.then_inc(sem("evacuated"), 1)

                def up_step(l, j, last):
                    taps(l, j, 0)
                    if not last:
                        lo(l, P_UP + 2, j)
                    taps(l, j, 1)
                    dve.drain()
                    dve.wait_ge(sem("silued"), l * (FT // 2) + j + 1)
                    dve.tensor_tensor(act_t[:, bass.ds(2 * j, 2), :], y_ab[:, 0, :, :], y_ab[:, 1, :, :],
                                      ALU.mult).then_inc(sem("hidden"), 1)
                    if not last:
                        lo(l, P_UP + 3, j)

                with dve.Fori(0, N_UP // 2 - 1) as j:
                    up_step(l, j, False)
                up_step(l, N_UP // 2 - 1, True)
                lo(l, P_DOWN)
                dve.drain()
                form_b(l, P_DOWN, N_DOWN, 1)
                post_norm(l, 1)

        @blk.tensor
        def _(pe):
            def three(dst, w, wl, xs, xl, start):
                pe.matmul(dst, w, xs, start=start, stop=False, skip_group_check=True)
                pe.matmul(dst, w, xl, start=False, stop=False, skip_group_check=True)
                return pe.matmul(dst, wl, xs, start=False, stop=True, skip_group_check=True)

            def pair_a(l, q, j, n):
                for s in range(4):
                    part_a(l, q, j, n, s)

            def part_a(l, q, j, n, s):
                if s == 0:
                    pe.wait_ge(sem("evacuated"), l * A_PAIRS + 2 * j + (n + 1))
                pe.wait_ge(lo_done, l * SUBS + 8 * j + (4 * q + s + 9))
                for i in range(2):
                    for kk in range(4):
                        k, c = 4 * s + kk, 256 * kk + 128 * i
                        ins = three(ps[:, q % 2, i * T:(i + 1) * T], w_hi[:, s, c:c + P], w_lo[:, s, c:c + P],
                                    h_hi[:, k, :], h_lo[:, k, :], k == 0 and i == 0)
                ins.then_inc(sub_used, 1)

            def gate_pair(l):
                pe.wait_ge(sem("evacuated"), l * A_PAIRS + 1)
                for s in range(4):
                    pe.wait_ge(lo_done, l * SUBS + (s + 9))
                    for t in range(TT):
                        for kk in range(4):
                            k, c = 4 * s + kk, NBA * kk
                            dst, tok = ps[:, 0, t * NBA:(t + 1) * NBA], slice(t * P, (t + 1) * P)
                            ins = three(dst, h_hi[:, k, tok], h_lo[:, k, tok], w_hi[:, s, c:c + NBA],
                                        w_lo[:, s, c:c + NBA], k == 0 and t == 0)
                    ins.then_inc(sub_used, 1)

            def pair_b(l, q, j, m, f, first, last):
                pe.wait_ge(sem("x_lo_done"), l * (N_OUT + N_DOWN) + f * N_OUT + 2 * j + (m + 1))
                for s in range(4):
                    pe.wait_ge(lo_done, l * SUBS + 8 * j + (4 * q + s + 9))
                    k = 2 * (q % 2) + s // 2
                    for t in range(TT):
                        tok = slice(t * P, (t + 1) * P)
                        for c in range(2):
                            dst = ps[:, 4 * t + 2 * (s % 2) + c, :]
                            w, wl = (v[:, s, 512 * c:512 * (c + 1)] for v in (w_hi, w_lo))
                            ins = three(dst, h_hi[:, k, tok], h_lo[:, k, tok], w, wl, first and s < 2)
                    ins.then_inc(sub_used, 1)

            def form_b(l, base, n, f):
                for i in range(2):
                    pair_b(l, base + i, 0, i, f, i == 0, False)
                with pe.Fori(0, n // 2 - 1) as j:
                    for i in range(2):
                        pair_b(l, base + 2 + i, j, 2 + i, f, False, False)

            def pre_norm(l, f):
                pe.wait_ge(sem("h_ready"), 4 * l + (2 * f + 2))
                for b in range(8):
                    for i in range(2):
                        for t in range(TT):
                            k = 2 * b + i
                            ins = pe.transpose(ps[:, b, i * T + t * P:i * T + (t + 1) * P],
                                               h_tok[:, t, k * P:(k + 1) * P], ident)
                    ins.then_inc(sem("h_turned"), 1)
                hold(pe, sem("h_lo_done"), 16 * l + (8 * f + 8))

            pe.nop().then_inc(sub_used, 4)
            pe.wait_ge(sem("const_in"), 16)
            with pe.Fori(0, DEPTH) as l:
                pe.wait_ge(sem("params_in"), l * (16 * N_PARAM_DMAS) + 16 * N_PARAM_DMAS)
                pe.wait_ge(sem("x_new"), 4 * l + 4)
                pe.transpose(ps[:, 0, 0:R_ONE], rows1[0:R_ONE, :], ident[0:R_ONE, 0:R_ONE])
                for b, n in ((0, P), (1, P), (2, FROWS - 2 * P)):
                    ins = pe.transpose(ps[:, 1, b * P:b * P + n], rows2[0:n, b, :], ident[0:n, 0:n])
                ins.then_inc(sem("params_turned"), 1)
                pe.wait_ge(sem("par_ready"), l + 1)
                pre_norm(l, 0)
                gate_pair(l)
                for q in range(1, P_GROUP):
                    pair_a(l, q, 0, q)
                    if q == 2:
                        gates_pe(pe, l)

                def more_of(q, j, n_parts):
                    def more(*parts):
                        for n in parts:
                            if n < n_parts:
                                part_a(l, q + n // 4, j, q + n // 4, n % 4)
                    return more

                hold(pe, sem("gate_exp"), l + 1)
                for kv in range(SWA_KV):
                    swa_pe(pe, l, kv, more_of(P_GROUP + 2 * kv, 0, 8))
                with pe.Fori(0, NG - 1) as g:
                    delta_pe(pe, l, g, more_of(P_GROUP + 4, 2 * g, 16))
                delta_pe(pe, l, NG - 1, more_of(P_POOL, 0, 8))
                pool_pe(pe, l)
                pe.wait_ge(sem("mixed"), l + 2)
                form_b(l, P_OUT, N_OUT, 0)
                pre_norm(l, 1)
                with pe.Fori(0, N_UP // 2) as j:
                    pair_a(l, P_UP, j, N_IN)
                    pair_a(l, P_UP + 1, j, N_IN + 1)
                pe.wait_ge(sem("evacuated"), l * A_PAIRS + (N_IN + N_UP + 2))
                form_b(l, P_DOWN, N_DOWN, 1)

N_PARAM_DMAS = 13
TWO_PI = (6.28125, 0.0019354820251464844, -1.7484555314695172e-07)
PI_IN = 3.1415925

_INS = ["x", "positions", "norm_mix_pre", "w_in", "dn_conv_w", "dn_a_log", "dn_dt_bias", "dn_norm_w", "pool_w",
        "pool_scale", "swa_sinks", "w_out", "norm_mix_post", "norm_ffn_pre", "ffn_w_up", "ffn_conv_w",
        "ffn_conv_b", "ffn_w_down", "norm_ffn_post"]


def kernel(**inputs):
    import concourse.bacc as bacc
    from concourse.bass_utils import run_bass_kernel_spmd

    nc = bacc.Bacc("TRN2", target_bir_lowering=False, num_devices=1)
    arrays, aps = {}, {}
    for name in _INS:
        v = np.ascontiguousarray(inputs[name])
        arrays["in_" + name] = v
        aps[name] = nc.dram_tensor("in_" + name, v.shape, mybir.dt.from_np(v.dtype), kind="ExternalInput").ap()
    arrays["in_consts"] = constants()
    aps["consts"] = nc.dram_tensor("in_consts", (P, C_ALL), F32, kind="ExternalInput").ap()
    out = nc.dram_tensor("out_x", (1, T, D), F32, kind="ExternalOutput").ap()
    trunk(nc, aps, out)
    r = run_bass_kernel_spmd(nc, [arrays], core_ids=[0])
    return r.results[0]["out_x"]
```
